# Optimizing a Trainium2 kernel written in Bass

```python
import math
import jax, jax.numpy as jnp
from jax import lax
import numpy as np

D_MODEL = 1024
BATCH = 1
SEQ = 256
DEPTH = 2

N_MIXERS = 2
ATTN_Q_HEADS = 16
ATTN_KV_HEADS = 2
ATTN_HEAD_DIM = 64
WINDOW = 128
ATTN_BLOCK = 128
RET_HEADS = 4
RET_QK_DIM = D_MODEL // RET_HEADS
RET_V_DIM = 2 * D_MODEL // RET_HEADS
RET_CHUNK = 128
ROPE_BASE = 10000.0
FFN_DIM = 2816
DEEPNORM_ALPHA = (2.0 * DEPTH) ** 0.25
DEEPNORM_BETA = (8.0 * DEPTH) ** -0.25
LN_EPS = 1e-5
GN_EPS = 1e-6
NEG_INF = -1e30

N_ATTN_LAYERS = (DEPTH + 1) // 2
N_RET_LAYERS = DEPTH // 2
ATTN_QKV_DIM = (ATTN_Q_HEADS + 2 * ATTN_KV_HEADS) * ATTN_HEAD_DIM
RET_PROJ_DIM = 2 * RET_HEADS * RET_QK_DIM + 2 * RET_HEADS * RET_V_DIM

kernel_name = "hybrid_swa_sink_retention_macaron_deepnorm"

def layer_norm(x, g, b):
    xf = x.astype(jnp.float32)
    mu = jnp.mean(xf, axis=-1, keepdims=True)
    var = jnp.mean(jnp.square(xf - mu), axis=-1, keepdims=True)
    y = (xf - mu) * lax.rsqrt(var + LN_EPS)
    return (y * g.astype(jnp.float32) + b.astype(jnp.float32)).astype(x.dtype)

def swiglu(x, w_gate_up, w_down):
    gate, up = jnp.split(x @ w_gate_up, 2, axis=-1)
    return (jax.nn.silu(gate) * up) @ w_down

def sliding_window_gqa(x, w_qkv, b_qkv, sinks, w_o, b_o):
    B, S, _ = x.shape
    H, KV, d, BLK = ATTN_Q_HEADS, ATTN_KV_HEADS, ATTN_HEAD_DIM, ATTN_BLOCK
    G = H // KV
    nb = S // BLK
    qkv = x @ w_qkv + b_qkv
    q = qkv[..., : H * d].reshape(B, nb, BLK, KV, G, d)
    k = qkv[..., H * d:(H + KV) * d].reshape(B, S, KV, d)
    v = qkv[..., (H + KV) * d:].reshape(B, S, KV, d)

    def band(t):
        prev = jnp.pad(t, ((0, 0), (BLK, 0), (0, 0), (0, 0)))[:, :S].reshape(B, nb, BLK, KV, d)
        cur = t.reshape(B, nb, BLK, KV, d)
        return jnp.concatenate([prev, cur], axis=2)

    kb, vb = band(k), band(v)
    scores = jnp.einsum('bnqkgd,bnjkd->bnkgqj', q, kb).astype(jnp.float32) * (d ** -0.5)
    qi = jnp.arange(BLK)[None, :, None]
    kj = jnp.arange(2 * BLK)[None, None, :]
    blk = jnp.arange(nb)[:, None, None]
    key_pos = blk * BLK - BLK + kj
    mask = (kj > qi + BLK - WINDOW) & (kj <= qi + BLK) & (key_pos >= 0)
    scores = jnp.where(mask[None, :, None, None], scores, NEG_INF)
    sink = jnp.broadcast_to(sinks.astype(jnp.float32).reshape(KV, G)[None, None, :, :, None, None],
                            scores.shape[:-1] + (1,))
    probs = jax.nn.softmax(jnp.concatenate([scores, sink], axis=-1), axis=-1)[..., :-1]
    o = jnp.einsum('bnkgqj,bnjkd->bnqkgd', probs.astype(x.dtype), vb).reshape(B, S, H * d)
    return o @ w_o + b_o

def rotary(t, pos):
    half = t.shape[-1] // 2
    freqs = 1.0 / (ROPE_BASE ** jnp.linspace(0.0, 1.0, half, dtype=jnp.float32))
    ang = pos[:, None] * freqs[None, :]
    cos = jnp.cos(ang)[None, :, None, :].astype(t.dtype)
    sin = jnp.sin(ang)[None, :, None, :].astype(t.dtype)
    t1, t2 = t[..., :half], t[..., half:]
    return jnp.concatenate([t1 * cos - t2 * sin, t1 * sin + t2 * cos], axis=-1)

def retention(x, w_qkvg, w_o):
    B, S, _ = x.shape
    H, dk, dv, C = RET_HEADS, RET_QK_DIM, RET_V_DIM, RET_CHUNK
    nc = S // C
    proj = x @ w_qkvg
    q = proj[..., : H * dk].reshape(B, S, H, dk)
    k = proj[..., H * dk: 2 * H * dk].reshape(B, S, H, dk)
    v = proj[..., 2 * H * dk: 2 * H * dk + H * dv].reshape(B, S, H, dv)
    g = proj[..., 2 * H * dk + H * dv:]
    pos = jnp.arange(S, dtype=jnp.float32)
    q = rotary(q, pos)
    k = rotary(k, pos) * (dk ** -0.5)

    log_gamma = jnp.log(1.0 - jnp.exp2(-5.0 - jnp.arange(H, dtype=jnp.float32)))
    idx = jnp.arange(C, dtype=jnp.float32)
    diff = idx[:, None] - idx[None, :]
    decay_in = jnp.where(diff >= 0, jnp.exp(jnp.maximum(diff, 0.0)[None] * log_gamma[:, None, None]), 0.0)
    q_decay = jnp.exp((idx + 1.0)[None, :] * log_gamma[:, None])
    k_decay = jnp.exp((C - 1.0 - idx)[None, :] * log_gamma[:, None])
    chunk_decay = jnp.exp(C * log_gamma).astype(x.dtype)

    qc = q.reshape(B, nc, C, H, dk)
    kc = k.reshape(B, nc, C, H, dk)
    vc = v.reshape(B, nc, C, H, dv)
    qk = jnp.einsum('bcnhd,bcmhd->bchnm', qc, kc) * decay_in.astype(x.dtype)[None, None]
    inner = jnp.einsum('bchnm,bcmhe->bcnhe', qk, vc)
    kd = kc * jnp.transpose(k_decay).astype(x.dtype)[None, None, :, :, None]
    kv = jnp.einsum('bcmhd,bcmhe->bchde', kd, vc)

    def step(state, kv_c):
        return state * chunk_decay[None, :, None, None] + kv_c, state

    _, prev = lax.scan(step, jnp.zeros((B, H, dk, dv), kv.dtype), jnp.moveaxis(kv, 1, 0))
    prev = jnp.moveaxis(prev, 0, 1)
    qd = qc * jnp.transpose(q_decay).astype(x.dtype)[None, None, :, :, None]
    cross = jnp.einsum('bcnhd,bchde->bcnhe', qd, prev)
    y = (inner + cross).reshape(B, S, H, dv)
    yf = y.astype(jnp.float32)
    mu = jnp.mean(yf, axis=-1, keepdims=True)
    var = jnp.mean(jnp.square(yf - mu), axis=-1, keepdims=True)
    y = ((yf - mu) * lax.rsqrt(var + GN_EPS)).astype(x.dtype).reshape(B, S, H * dv)
    return (jax.nn.silu(g) * y) @ w_o

def setup_inputs(seed: int = 0) -> dict:
    key = jax.random.key(seed)
    ks = jax.random.split(key, 14)
    f32 = jnp.float32
    D, F = D_MODEL, FFN_DIM
    nrm = lambda k, shape, s: jax.random.normal(k, shape, f32) * s
    return {
        "x": nrm(ks[0], (BATCH, SEQ, D), 1.0),
        "ln_g": 1.0 + nrm(ks[1], (DEPTH, 3, D), 0.02),
        "ln_b": nrm(ks[2], (DEPTH, 3, D), 0.02),
        "ffn1_w_gate_up": nrm(ks[3], (DEPTH, D, 2 * F), D ** -0.5),
        "ffn1_w_down": nrm(ks[4], (DEPTH, F, D), F ** -0.5 * DEEPNORM_BETA),
        "ffn2_w_gate_up": nrm(ks[5], (DEPTH, D, 2 * F), D ** -0.5),
        "ffn2_w_down": nrm(ks[6], (DEPTH, F, D), F ** -0.5 * DEEPNORM_BETA),
        "attn_w_qkv": nrm(ks[7], (N_ATTN_LAYERS, D, ATTN_QKV_DIM), D ** -0.5),
        "attn_b_qkv": nrm(ks[8], (N_ATTN_LAYERS, ATTN_QKV_DIM), 0.02),
        "attn_sinks": nrm(ks[9], (N_ATTN_LAYERS, ATTN_Q_HEADS), 1.0),
        "attn_w_o": nrm(ks[10], (N_ATTN_LAYERS, ATTN_Q_HEADS * ATTN_HEAD_DIM, D),
                        (ATTN_Q_HEADS * ATTN_HEAD_DIM) ** -0.5 * DEEPNORM_BETA),
        "attn_b_o": nrm(ks[11], (N_ATTN_LAYERS, D), 0.02),
        "ret_w_qkvg": nrm(ks[12], (N_RET_LAYERS, D, RET_PROJ_DIM), D ** -0.5),
        "ret_w_o": nrm(ks[13], (N_RET_LAYERS, RET_HEADS * RET_V_DIM, D),
                       (RET_HEADS * RET_V_DIM) ** -0.5 * DEEPNORM_BETA),
    }

def reference(x, ln_g, ln_b, ffn1_w_gate_up, ffn1_w_down, ffn2_w_gate_up, ffn2_w_down,
              attn_w_qkv, attn_b_qkv, attn_sinks, attn_w_o, attn_b_o, ret_w_qkvg, ret_w_o):
    a = DEEPNORM_ALPHA
    for i in range(DEPTH):
        x = layer_norm(a * x + 0.5 * swiglu(x, ffn1_w_gate_up[i], ffn1_w_down[i]), ln_g[i, 0], ln_b[i, 0])
        j = i // N_MIXERS
        if i % N_MIXERS == 0:
            mix = sliding_window_gqa(x, attn_w_qkv[j], attn_b_qkv[j], attn_sinks[j], attn_w_o[j], attn_b_o[j])
        else:
            mix = retention(x, ret_w_qkvg[j], ret_w_o[j])
        x = layer_norm(a * x + mix, ln_g[i, 1], ln_b[i, 1])
        x = layer_norm(a * x + 0.5 * swiglu(x, ffn2_w_gate_up[i], ffn2_w_down[i]), ln_g[i, 2], ln_b[i, 2])
    return x


_drawn_inputs = setup_inputs


def setup_inputs(seed=0):
    import zlib

    import numpy as np

    out = dict(_drawn_inputs(seed))
    spreads = {}
    factors = {'attn_b_qkv': 7.742, 'attn_sinks': 5.93, 'attn_b_o': 3.71}
    for name, (base, spread) in spreads.items():
        noise = np.random.default_rng([zlib.crc32(name.encode()), seed]).standard_normal(out[name].shape)
        drawn = base * np.exp(spread * noise) if base else spread * noise
        out[name] = __import__('jax').numpy.asarray(drawn.astype(out[name].dtype))
    for name, factor in factors.items():
        out[name] = (out[name] * factor).astype(out[name].dtype)
    return out
```

```python
import concourse.bass as bass
from concourse import mybir
from contextlib import ExitStack

P = 128
D = 1024
SEQ = 256
NT = SEQ // P
KD = D // P
FFN = 2816
HC = 256
NCH = FFN // HC
KF = FFN // P
NH, NKV, DH = 16, 2, 64
NB = NH // 2
RH, RQ, RV = 4, 256, 512
SLOT = 2048
RING = 4
BANK = 512
ALPHA = (2.0 * 2) ** 0.25
LN_EPS, GN_EPS = 1e-5, 1e-6

FFN_SLOTS = 2 * NCH + KF // 2
ATT_SLOTS = 1 + 4 + 4
RET_SLOTS = 24 + 8
FFN_BASE = [0, FFN_SLOTS + ATT_SLOTS, 2 * FFN_SLOTS + ATT_SLOTS, 3 * FFN_SLOTS + ATT_SLOTS + RET_SLOTS]
ATT_BASE = FFN_SLOTS
RET_BASE = 3 * FFN_SLOTS + ATT_SLOTS
N_SLOTS = 4 * FFN_SLOTS + ATT_SLOTS + RET_SLOTS
FFN_NORM = [0, 2, 3, 5]
ATT_NORM, RET_NORM = 1, 4
N_NORMS = 6
END_SLOT = [FFN_SLOTS, ATT_BASE + ATT_SLOTS, FFN_BASE[1] + FFN_SLOTS, FFN_BASE[2] + FFN_SLOTS,
            RET_BASE + RET_SLOTS, N_SLOTS]


def trunk(nc, x, weights, norm_rows, norm_cols, att_cols, sinks, att_rows, ident_in, mask_in, rope_in, decay_in, out):
    f32 = mybir.dt.float32
    f32r = mybir.dt.float32r
    ALU = mybir.AluOpType
    ACT = mybir.ActivationFunctionType
    AX = mybir.AxisListType

    ctx = ExitStack()
    with ctx:
        def sb(name, shape, dt=f32, within=ctx):
            return within.enter_context(nc.sbuf_tensor(name, shape, dt))

        def sem(name):
            return ctx.enter_context(nc.semaphore(name))

        w_raw = sb("w_raw", [P, RING, SLOT])
        w_hi = sb("w_hi", [P, RING, SLOT], f32r)
        w_lo = sb("w_lo", [P, RING, SLOT], f32r)
        xT_hi = sb("xT_hi", [P, KD, SEQ], f32r)
        xT_lo = sb("xT_lo", [P, KD, SEQ], f32r)
        x_nat = sb("x_nat", [P, NT, D])
        z = sb("z", [P, NT, D])
        xT_full = sb("xT_full", [P, KD, P])
        gain_row = sb("gain_row", [P, D])
        bias_row = sb("bias_row", [P, D])
        cols = sb("cols", [P, 2, N_NORMS, KD])
        stats = sb("stats", [P, NT, 2, 6])
        moments = sb("moments", [P, NT, 2])
        rstd = sb("rstd", [P, NT, 1])
        eps_pow = sb("eps_pow", [P, 3])
        ident = sb("ident", [P, P])
        gn_stats = sb("gn_stats", [P, NT, 6])
        gn_moments = sb("gn_moments", [P, NT, 2])
        gn_rstd = sb("gn_rstd", [P, NT, 1])

        def ffn_tensors(f):
            with ExitStack() as r:
                return [sb(f"{n}{f}", s, d, r) for n, s, d in (
                    ("hT_hi", [P, KF, SEQ], f32r), ("hT_lo", [P, KF, SEQ], f32r),
                    ("silu_gate", [P, NT, HC], f32), ("h_nat", [P, NT, HC], f32))]

        ffn_bufs = [ffn_tensors(f) for f in range(4)]
        with ExitStack() as r:
            oT_hi = sb("oT_hi", [P, NB, SEQ], f32r, r)
            oT_lo = sb("oT_lo", [P, NB, SEQ], f32r, r)
            q_nat = sb("q_nat", [P, NT, BANK], f32, r)
            qT = sb("qT", [P, NB, SEQ], f32, r)
            k_twice = sb("k_twice", [P, NT, NKV, 2, DH], f32, r)
            kT = sb("kT", [P, NKV, 2, SEQ], f32, r)
            v_nat = sb("v_nat", [P, NT, NKV * DH], f32, r)
            probs = sb("probs", [P, 2, 768], f32, r)
            pT1 = sb("pT1", [P, 2, 2, 4, P], f32, r)
            pT0 = sb("pT0", [P, 2, 4, P], f32, r)
            mask = sb("mask", [P, 2 * P], f32, r)
            bo_row = sb("bo_row", [P, D], f32, r)
            bv_row = sb("bv_row", [P, NKV * DH], f32, r)
            bq_col = sb("bq_col", [P, NB + NKV], f32, r)
            sink = sb("sink", [P, NB, 4], f32, r)
            peak = sb("peak", [P, 2, 4], f32, r)
            peak_s = sb("peak_s", [P, 2, 4], f32, r)
            neg_peak = sb("neg_peak", [P, 2, 4], f32, r)
            sink_less = sb("sink_less", [P, 2, 4], f32, r)
            sink_exp = sb("sink_exp", [P, 2, 4], f32, r)
            sums = sb("sums", [P, 2, 4], f32, r)
            total = sb("total", [P, 2, 4], f32, r)
            inv = sb("inv", [P, 2, 4], f32, r)
        with ExitStack() as r:
            scT = sb("scT", [P, RH, 384], f32, r)
            rv = sb("rv", [P, NT, RV], f32, r)
            silu_g = sb("silu_g", [P, NT, RV], f32, r)
            y_nat = sb("y_nat", [P, NT, RV], f32, r)
            decay = sb("decay", [P, RH, 384], f32, r)
            rope = sb("rope", [P, NT, 2, P], f32, r)
            with ExitStack() as early:
                rqkT = sb("rqkT", [P, 16, SEQ], f32, early)
                by_cos = sb("by_cos", [P, BANK], f32, early)
                by_sin = sb("by_sin", [P, BANK], f32, early)
                rot = sb("rot", [P, NT, BANK], f32, early)
            gT_hi = sb("gT_hi", [P, 16, SEQ], f32r, r)
            gT_lo = sb("gT_lo", [P, 16, SEQ], f32r, r)

        ps = [ctx.enter_context(nc.psum_tensor(f"bank{b}", [P, BANK], f32)) for b in range(8)]
        Y = [[ps[4 + 2 * t + n] for n in range(2)] for t in range(NT)]

        raw_loaded = [sem(f"raw_loaded{i}") for i in range(RING)]
        x_loaded = sem("x_loaded")
        consts_loaded = sem("consts_loaded")
        rows_loaded = sem("rows_loaded")
        att_consts = sem("att_consts")
        ret_consts = sem("ret_consts")
        hi_ready = sem("hi_ready")
        lo_ready = sem("lo_ready")
        slots_used = sem("slots_used")
        y_half_ready = sem("y_half_ready")
        sums_ready = sem("sums_ready")
        stats_ready = sem("stats_ready")
        var_ready = sem("var_ready")
        rstd_ready = sem("rstd_ready")
        xhat_ready = sem("xhat_ready")
        xT_psum = sem("xT_psum")
        xT_a_full = sem("xT_a_full")
        xT_b_full = sem("xT_b_full")
        xhi_ready = sem("xhi_ready")
        xT_ready = sem("xT_ready")
        x_scaled = sem("x_scaled")
        xnat_ready = sem("xnat_ready")
        res_ready = sem("res_ready")
        eps_ready = sem("eps_ready")
        silu_ready = sem("silu_ready")
        h_ready = sem("h_ready")
        hT_psum = sem("hT_psum")
        hT_hi_ready = sem("hT_hi_ready")
        hT_ready = sem("hT_ready")
        kz_ready = sem("kz_ready")
        kv_nat = sem("kv_nat")
        kT_psum = sem("kT_psum")
        kT_ready = sem("kT_ready")
        q_nat_ready = sem("q_nat_ready")
        qT_psum = sem("qT_psum")
        qT_ready = sem("qT_ready")
        scores_ready = sem("scores_ready")
        masked = sem("masked")
        soft_step = sem("soft_step")
        peaks_ready = sem("peaks_ready")
        exps_ready = sem("exps_ready")
        probs_ready = sem("probs_ready")
        pT_psum = sem("pT_psum")
        pT1_ready = sem("pT1_ready")
        pT0_ready = sem("pT0_ready")
        o_psum = sem("o_psum")
        oT_hi_ready = sem("oT_hi_ready")
        oT_ready = sem("oT_ready")
        rot_step = sem("rot_step")
        rot_ready = sem("rot_ready")
        rqkT_psum = sem("rqkT_psum")
        rqkT_ready = sem("rqkT_ready")
        scT_psum = sem("scT_psum")
        scT_ready = sem("scT_ready")
        rv_ready = sem("rv_ready")
        ry_psum = sem("ry_psum")
        gn_step = sem("gn_step")
        gn_stats_ready = sem("gn_stats_ready")
        gn_var = sem("gn_var")
        gn_rstd_ready = sem("gn_rstd_ready")
        yn_ready = sem("yn_ready")
        silu_g_ready = sem("silu_g_ready")
        gated_ready = sem("gated_ready")
        gT_psum = sem("gT_psum")
        gT_hi_ready = sem("gT_hi_ready")
        gT_ready = sem("gT_ready")
        out_step = sem("out_step")
        out_ready = sem("out_ready")
        out_stored = sem("out_stored")

        def used(s):
            return s + 1

        block = ctx.enter_context(nc.Block())

        @block.sync
        def _(sp):
            def load(s, i=0):
                if s >= RING:
                    sp.wait_ge(lo_ready, s - RING + 1 + RING * i)
                sp.dma_start(w_raw[:, s % RING, :], weights[bass.ds((s + RING * i) * P, P), :]).then_inc(raw_loaded[s % RING], 16)

            sp.dma_start(ident[:], ident_in).then_inc(consts_loaded, 16)
            for t in range(NT):
                sp.dma_start(x_nat[:, t, :], x[t * P:(t + 1) * P, :]).then_inc(x_loaded, 16)
            for s in range(RING):
                load(s)
            sp.dma_start(cols[:], norm_cols).then_inc(consts_loaded, 16)
            with sp.Fori(0, N_SLOTS // RING - 1) as i:
                for s in range(RING, 2 * RING):
                    load(s, i)
            for s in range(N_SLOTS // RING * RING, N_SLOTS):
                load(s)
            for t in range(NT):
                for n in range(2):
                    sp.wait_ge(out_ready, 2 * t + n + 1)
                    sp.dma_start(out[t * P:(t + 1) * P, n * BANK:(n + 1) * BANK],
                                 z[:, t, n * BANK:(n + 1) * BANK]).then_inc(out_stored, 16)
            sp.wait_ge(out_stored, 16 * 2 * NT)

        @block.tensor
        def _(pe):
            def three(bank, hi, lo, whi, wlo, start, stop):
                nc.tensor.matmul(bank, hi, whi, start=start, stop=False)
                nc.tensor.matmul(bank, hi, wlo, start=False, stop=False)
                return nc.tensor.matmul(bank, lo, whi, start=False, stop=stop)

            def part(s, t, n_k, width, act_hi, act_lo, k0, banks, first, last):
                done = None
                tok = slice(t * P, (t + 1) * P)
                for k in range(n_k):
                    for n, bank in enumerate(banks):
                        w = slice(k * width + n * BANK, k * width + min(width, (n + 1) * BANK))
                        done = three(bank[:, 0:min(width, BANK)], act_hi[:, k0 + k, tok], act_lo[:, k0 + k, tok],
                                     w_hi[:, s % RING, w], w_lo[:, s % RING, w],
                                     first and k == 0, last and k == n_k - 1)
                return done

            def wait_slot(s, i=0):
                pe.wait_ge(lo_ready, s + 1 + RING * i)

            def x_transposes(number, t, src):
                for half in range(2):
                    if number >= NT:
                        pe.wait_ge(xhat_ready, 2 * (number - NT) + half + 1)
                    for k in range(4):
                        f = slice((4 * half + k) * P, (4 * half + k + 1) * P)
                        done = nc.tensor.transpose(ps[2 * half + t][:, k * P:(k + 1) * P], src[:, t, f], ident[:])
                    done.then_inc(xT_psum, 1)

            def opening(base, spec, norm):
                for t in range(NT):
                    if t == 1:
                        x_transposes(norm_number(norm, 1), 1, x_nat if norm < 0 else z)
                    for j, (n_k, width, k0, banks, first, last) in enumerate(spec):
                        if t == 0:
                            wait_slot(base + j)
                        if j == 0:
                            pe.wait_ge(xT_ready, norm_number(norm, t) + 1)
                        done = part(base + j, t, n_k, width, xT_hi, xT_lo, k0, [banks[t]], first, last)
                        if t == 1:
                            done.then_inc(slots_used, 1)

            def norm_number(norm, t):
                return NT * (norm + 1) + t

            def closing(base, act_hi, act_lo, k0, norm):
                for t in range(NT):
                    for j in range(2):
                        if t == 0:
                            wait_slot(base + j)
                        done = part(base + j, t, 2, D, act_hi, act_lo, k0 + 2 * j, Y[t], False, j == 1)
                        if t == 1:
                            done.then_inc(slots_used, 1)
                    if t == 0:
                        done.then_inc(y_half_ready, 1)
                if norm < N_NORMS - 1:
                    x_transposes(norm_number(norm, 0), 0, z)

            def output_slot(s, act_hi, act_lo, k0, first):
                wait_slot(s)
                for t in range(NT):
                    done = part(s, t, 2, D, act_hi, act_lo, k0, Y[t], first, False)
                done.then_inc(slots_used, 1)

            def half_chunk(s, half, banks, i=0):
                wait_slot(s, i)
                for t in range(NT):
                    done = part(s, t, 4, BANK, xT_hi, xT_lo, 4 * half, [banks[t]], half == 0, half == 1)
                done.then_inc(slots_used, 1)

            def ffn(f):
                base = FFN_BASE[f]
                hT_hi, hT_lo, _, h_nat = ffn_bufs[f]
                pair = [[ps[0], ps[1]], [ps[2], ps[3]]]

                def h_transposes(c, bank, i=0):
                    pe.wait_ge(h_ready, 2 * (NCH * f + c) + 2 + 4 * i)
                    for b in range(2):
                        for t in range(NT):
                            done = nc.tensor.transpose(bank[:, (2 * b + t) * P:(2 * b + t + 1) * P],
                                                       h_nat[:, t, b * P:(b + 1) * P], ident[:])
                    done.then_inc(hT_psum, 1)

                opening(base, [(4, BANK, 0, pair[0], True, False), (4, BANK, 4, pair[0], False, True),
                               (4, BANK, 0, pair[1], True, False)], FFN_NORM[f] - 1)
                half_chunk(base + 3, 1, pair[1])
                h_transposes(0, ps[4])
                with pe.Fori(0, 4) as i:
                    for c in (2, 3):
                        pe.wait_ge(h_ready, 2 * (NCH * f + c - 2) + 2 + 4 * i)
                        half_chunk(base + 2 * c, 0, pair[c % 2], i)
                        h_transposes(c - 1, ps[4 + (c - 1) % 2], i)
                        half_chunk(base + 2 * c + 1, 1, pair[c % 2], i)
                pe.wait_ge(h_ready, 2 * (NCH * f + NCH - 3) + 2)
                half_chunk(base + 2 * NCH - 2, 0, pair[0])
                h_transposes(NCH - 2, ps[5])
                half_chunk(base + 2 * NCH - 1, 1, pair[0])
                down = base + 2 * NCH
                for d in range(NCH - 2):
                    pe.wait_ge(hT_ready, NCH * f + NCH - 1)
                    output_slot(down + d, hT_hi, hT_lo, 2 * d, d == 0)
                    if d == 0:
                        h_transposes(NCH - 1, ps[0])
                pe.wait_ge(hT_ready, NCH * f + NCH)
                closing(down + NCH - 2, hT_hi, hT_lo, 2 * (NCH - 2), FFN_NORM[f])

            def attention():
                base = ATT_BASE
                opening(base, [(KD, 256, 0, [ps[0], ps[1]], True, True),
                               (4, BANK, 0, [ps[2], ps[3]], True, False),
                               (4, BANK, 4, [ps[2], ps[3]], False, True)], ATT_NORM - 1)
                half_chunk(base + 3, 0, [ps[6], ps[7]])
                pe.wait_ge(kv_nat, NT)
                for g in range(NKV):
                    for t in range(NT):
                        done = nc.tensor.transpose(ps[0][:, (2 * g + t) * P:(2 * g + t + 1) * P],
                                                   k_twice[:, t, g, :, :].rearrange("p a b -> p (a b)"), ident[:])
                done.then_inc(kT_psum, 1)

                def q_transposes(n):
                    pe.wait_ge(q_nat_ready, n + 1)
                    if n:
                        pe.wait_ge(qT_ready, 1)
                    for b in range(4):
                        for t in range(NT):
                            c = (2 * (b % 2) + t) * P
                            done = nc.tensor.transpose(ps[2 + b // 2][:, c:c + P], q_nat[:, t, b * P:(b + 1) * P], ident[:])
                    done.then_inc(qT_psum, 1)

                def scores(b):
                    bank1, bank0 = ((ps[4], ps[5]), (ps[0], ps[1]))[b % 2]
                    if b == 0:
                        pe.wait_ge(kT_ready, 1)
                    if b % 4 == 0:
                        pe.wait_ge(qT_ready, b // 4 + 1)
                    if b >= 2:
                        pe.wait_ge(masked, b - 1)
                    g = b // 4
                    nc.tensor.matmul(bank1[:], qT[:, b, P:2 * P], kT[:, g, :, :].rearrange("p j k -> p (j k)"),
                                     start=True, stop=True)
                    nc.tensor.matmul(bank0[:, 0:2 * P], qT[:, b, 0:P], kT[:, g, :, 0:P],
                                     start=True, stop=True).then_inc(scores_ready, 1)

                def p_transposes(b):
                    pe.wait_ge(probs_ready, b + 1)
                    if b == 0:
                        pe.wait_ge(qT_ready, 2)
                    else:
                        pe.wait_ge(pT1_ready, b)
                        pe.wait_ge(pT0_ready, b)
                    for j in range(2):
                        for kb in range(2):
                            nc.tensor.transpose(ps[2][:, (2 * j + kb) * P:(2 * j + kb + 1) * P],
                                                probs[:, b % 2, j * 256 + kb * P:j * 256 + (kb + 1) * P], ident[:])
                    for j in range(2):
                        done = nc.tensor.transpose(ps[3][:, j * P:(j + 1) * P],
                                                   probs[:, b % 2, 512 + j * P:512 + (j + 1) * P], ident[:])
                    done.then_inc(pT_psum, 1)

                def values(g):
                    pe.wait_ge(pT1_ready, 4 * g + 4)
                    pe.wait_ge(pT0_ready, 4 * g + 4)
                    if g:
                        pe.wait_ge(oT_ready, g)
                    for j in range(2):
                        rows = slice(j * DH, (j + 1) * DH)
                        v = [v_nat[:, t, g * DH:(g + 1) * DH] for t in range(NT)]
                        for kb in range(2):
                            nc.tensor.matmul(ps[6][rows, :], v[kb], pT1[:, kb, j, :, :].rearrange("p b q -> p (b q)"),
                                             start=kb == 0, stop=kb == 1)
                        done = nc.tensor.matmul(ps[7][rows, :], v[0], pT0[:, j, :, :].rearrange("p b q -> p (b q)"),
                                                start=True, stop=True)
                    done.then_inc(o_psum, 1)

                q_transposes(0)
                half_chunk(base + 4, 1, [ps[6], ps[7]])
                for b in range(NB + 2):
                    if b < NB:
                        scores(b)
                    if b == 1:
                        q_transposes(1)
                    if b >= 2:
                        p_transposes(b - 2)
                    if b == 6:
                        values(0)
                values(1)
                pe.wait_ge(oT_ready, 2)
                for d in range(2):
                    output_slot(base + 5 + d, oT_hi, oT_lo, 2 * d, d == 0)
                closing(base + 7, oT_hi, oT_lo, 4, ATT_NORM)

            def retention():
                base = RET_BASE
                pair = [[ps[0], ps[1]], [ps[2], ps[3]]]

                def rot_transposes(c):
                    pe.wait_ge(rot_ready, 2 * c + 2)
                    if c:
                        pe.wait_ge(rqkT_ready, c)
                    for b in range(4):
                        for t in range(NT):
                            col = (2 * (b % 2) + t) * P
                            done = nc.tensor.transpose(ps[4 + b // 2][:, col:col + P], rot[:, t, b * P:(b + 1) * P], ident[:])
                    done.then_inc(rqkT_psum, 1)

                def ret_scores(h):
                    bank = ps[6 + h % 2]
                    if h >= 2:
                        pe.wait_ge(scT_ready, h - 1)
                    for half in range(2):
                        nc.tensor.matmul(bank[:, 0:256], rqkT[:, 8 + 2 * h + half, 0:P], rqkT[:, 2 * h + half, :],
                                         start=half == 0, stop=half == 1)
                    for half in range(2):
                        done = nc.tensor.matmul(bank[:, 256:384], rqkT[:, 8 + 2 * h + half, P:SEQ],
                                                rqkT[:, 2 * h + half, P:SEQ], start=half == 0, stop=half == 1)
                    done.then_inc(scT_psum, 1)

                def ret_values(h):
                    pe.wait_ge(scT_ready, RH)
                    pe.wait_ge(rv_ready, 2 * h + 2)
                    if h:
                        pe.wait_ge(yn_ready, 2 * h)
                    nc.tensor.matmul(ps[6][:], scT[:, h, 0:P], rv[:, 0, :], start=True, stop=True)
                    nc.tensor.matmul(ps[7][:], scT[:, h, P:2 * P], rv[:, 0, :], start=True, stop=False)
                    nc.tensor.matmul(ps[7][:], scT[:, h, 2 * P:3 * P], rv[:, 1, :], start=False, stop=True).then_inc(ry_psum, 1)

                def gated_transposes(h, banks):
                    pe.wait_ge(gated_ready, 2 * h + 2)
                    if h:
                        pe.wait_ge(gT_ready, h)
                    for b in range(4):
                        for t in range(NT):
                            col = (2 * (b % 2) + t) * P
                            done = nc.tensor.transpose(banks[b // 2][:, col:col + P], y_nat[:, t, b * P:(b + 1) * P], ident[:])
                    done.then_inc(gT_psum, 1)

                opening(base, [(4, BANK, 0, pair[0], True, False), (4, BANK, 4, pair[0], False, True),
                               (4, BANK, 0, pair[1], True, False)], RET_NORM - 1)
                half_chunk(base + 3, 1, pair[1])
                rot_transposes(0)
                for c in (2, 3):
                    pe.wait_ge(rot_ready, 2 * (c - 2) + 2)
                    half_chunk(base + 2 * c, 0, pair[c % 2])
                    rot_transposes(c - 1)
                    half_chunk(base + 2 * c + 1, 1, pair[c % 2])
                for h in range(RH):
                    if h == 0:
                        pe.wait_ge(rot_ready, 6)
                    else:
                        pe.wait_ge(rv_ready, 2 * h)
                    half_chunk(base + 8 + 4 * h, 0, pair[0])
                    if h == 0:
                        rot_transposes(3)
                    else:
                        gated_transposes(h - 1, [ps[4], ps[5]])
                    half_chunk(base + 9 + 4 * h, 1, pair[0])
                    if h == 0:
                        pe.wait_ge(rqkT_ready, 4)
                        for head in range(RH):
                            ret_scores(head)
                        pe.wait_ge(rot_ready, 8)
                    else:
                        pe.wait_ge(silu_g_ready, 2 * h)
                    half_chunk(base + 10 + 4 * h, 0, pair[1])
                    ret_values(h)
                    half_chunk(base + 11 + 4 * h, 1, pair[1])
                for d in range(6):
                    pe.wait_ge(gT_ready, RH - 1)
                    pe.wait_ge(yn_ready, 2 * RH)
                    output_slot(base + 24 + d, gT_hi, gT_lo, 2 * d, d == 0)
                    if d == 0:
                        gated_transposes(3, [ps[0], ps[1]])
                pe.wait_ge(gT_ready, RH)
                closing(base + 30, gT_hi, gT_lo, 12, RET_NORM)

            pe.wait_ge(consts_loaded, 16)
            pe.wait_ge(x_loaded, 32)
            x_transposes(0, 0, x_nat)
            ffn(0)
            attention()
            ffn(1)
            ffn(2)
            retention()
            ffn(3)

        @block.scalar
        def _(act):
            def split_hi(s, i=0):
                if s >= N_SLOTS:
                    return
                act.wait_ge(raw_loaded[s % RING], 16 * (s // RING + 1) + 16 * i)
                if s >= RING:
                    act.wait_ge(slots_used, used(s - RING) + RING * i)
                nc.scalar.activation(w_hi[:, s % RING, :], w_raw[:, s % RING, :], ACT.Copy).then_inc(hi_ready, 1)

            def first_x_hi(t):
                for half in range(2):
                    act.wait_ge(xT_psum, 2 * t + half + 1)
                    nc.scalar.activation(xT_hi[:, 4 * half:4 * half + 4, t * P:(t + 1) * P],
                                         ps[2 * half + t][:].rearrange("p (k q) -> p k q", k=4), ACT.Copy).then_inc(xhi_ready, 1)

            def norm_hi(norm, t):
                number = NT * (norm + 1) + t
                act.wait_ge(xT_psum, 2 * number + 2)
                act.wait_ge(xT_ready, number)
                for k in range(4, 8):
                    done = nc.scalar.activation(xT_full[:, k, :], ps[2 + t][:, (k - 4) * P:(k - 3) * P], ACT.Identity,
                                                bias=cols[:, 1, norm, k:k + 1], scale=cols[:, 0, norm, k:k + 1])
                done.then_inc(xT_b_full, 1)
                for half in range(2):
                    k = slice(4 * half, 4 * half + 4)
                    act.wait_ge(*((xT_a_full, NT * norm + t + 1) if half == 0 else (xT_b_full, NT * norm + t + 1)))
                    nc.scalar.activation(xT_hi[:, k, t * P:(t + 1) * P], xT_full[:, k, :], ACT.Copy).then_inc(xhi_ready, 1)

            def ffn(f):
                base = FFN_BASE[f]
                hT_hi, _, silu_gate, _ = ffn_bufs[f]

                def silu(c, i=0):
                    act.wait_ge(slots_used, used(base + 2 * c + 1) + RING * i)
                    if f or c:
                        act.wait_ge(h_ready, 2 * (NCH * f + c) + 4 * i)
                    for t in range(NT):
                        nc.scalar.activation(silu_gate[:, t, :], ps[2 * (c % 2) + t][:, 0:HC], ACT.Silu).then_inc(silu_ready, 1)

                def hidden_hi(c, bank, i=0):
                    act.wait_ge(hT_psum, NCH * f + c + 1 + 2 * i)
                    at = bass.ds(2 * c + 4 * i, 2) if not isinstance(i, int) else slice(2 * c, 2 * c + 2)
                    nc.scalar.activation(hT_hi[:, at, :], bank[:].rearrange("p (b q) -> p b q", b=2), ACT.Copy).then_inc(hT_hi_ready, 1)

                split_hi(base + 3)
                split_hi(base + 4)
                silu(0)
                split_hi(base + 5)
                split_hi(base + 6)
                hidden_hi(0, ps[4])
                with act.Fori(0, 4) as i:
                    for c in (2, 3):
                        silu(c - 1, i)
                        split_hi(base + 2 * c + 3, i)
                        hidden_hi(c - 1, ps[4 + (c - 1) % 2], i)
                        split_hi(base + 2 * c + 4, i)
                silu(NCH - 2)
                split_hi(base + 2 * NCH + 1)
                hidden_hi(NCH - 2, ps[5])
                split_hi(base + 2 * NCH + 2)
                silu(NCH - 1)
                split_hi(base + 2 * NCH + 3)
                hidden_hi(NCH - 1, ps[0])
                for s in range(2 * NCH + 4, FFN_SLOTS + 2):
                    split_hi(base + s)
                ending(FFN_NORM[f])

            def ending(norm):
                if norm == N_NORMS - 1:
                    return
                split_hi(END_SLOT[norm] + 2)
                norm_hi(norm, 0)
                norm_hi(norm, 1)

            def attention():
                base = ATT_BASE

                def q_copy(n):
                    act.wait_ge(slots_used, used(base + (2, 4)[n]))
                    if n:
                        act.wait_ge(qT_psum, 1)
                    for t in range(NT):
                        done = nc.scalar.activation(q_nat[:, t, :], ps[(2, 6)[n] + t][:], ACT.Copy)
                    done.then_inc(q_nat_ready, 1)

                def exps(b):
                    act.wait_ge(peaks_ready, b + 1)
                    for i, (c, w) in enumerate(((0, 256), (256, 256), (512, P), (640, P))):
                        nc.scalar.activation(probs[:, b % 2, c:c + w], probs[:, b % 2, c:c + w], ACT.Exp,
                                             bias=neg_peak[:, b % 2, i:i + 1], accum_out=sums[:, b % 2, i:i + 1])
                    nc.scalar.activation(sink_exp[:, b % 2, :], sink_less[:, b % 2, :], ACT.Exp).then_inc(exps_ready, 1)

                def pT1_copy(b):
                    act.wait_ge(pT_psum, b + 1)
                    if b == 4:
                        act.wait_ge(o_psum, 1)
                    nc.scalar.activation(pT1[:, :, :, b % 4, :].rearrange("p k j q -> p j k q"),
                                         ps[2][:].rearrange("p (j k q) -> p j k q", j=2, k=2), ACT.Copy).then_inc(pT1_ready, 1)

                def o_hi(g):
                    act.wait_ge(o_psum, g + 1)
                    for t in range(NT):
                        nc.scalar.activation(oT_hi[:, 4 * g:4 * g + 4, t * P:(t + 1) * P],
                                             ps[7 - t][:].rearrange("p (b q) -> p b q", b=4), ACT.Copy).then_inc(oT_hi_ready, 1)

                split_hi(base + 3)
                q_copy(0)
                split_hi(base + 4)
                act.wait_ge(kT_psum, 1)
                act.wait_ge(kz_ready, 1)
                act.wait_ge(att_consts, 16 * 5)
                for g in range(NKV):
                    for j in range(2):
                        rows = slice(j * DH, (j + 1) * DH)
                        done = nc.scalar.activation(kT[rows, g, j, :], ps[0][rows, g * SEQ:(g + 1) * SEQ], ACT.Identity,
                                                    bias=bq_col[rows, NB + g:NB + g + 1])
                done.then_inc(kT_ready, 1)
                split_hi(base + 5)
                split_hi(base + 6)
                q_copy(1)
                for b in range(NB + 2):
                    if b < NB:
                        exps(b)
                    if b >= 2:
                        pT1_copy(b - 2)
                    if b == 3:
                        split_hi(base + 7)
                    if b == 5:
                        split_hi(base + 8)
                    if b == 7:
                        o_hi(0)
                o_hi(1)
                split_hi(base + 9)
                split_hi(base + 10)
                ending(ATT_NORM)

            def retention():
                base = RET_BASE

                def rqk_copy(c):
                    act.wait_ge(rqkT_psum, c + 1)
                    for half in range(2):
                        done = nc.scalar.activation(rqkT[:, 4 * c + 2 * half:4 * c + 2 * half + 2, :],
                                                    ps[4 + half][:].rearrange("p (b q) -> p b q", b=2), ACT.Copy)
                    done.then_inc(rqkT_ready, 1)

                def v_copy(h):
                    act.wait_ge(slots_used, used(base + 9 + 4 * h))
                    if h:
                        act.wait_ge(ry_psum, h)
                    for t in range(NT):
                        nc.scalar.activation(rv[:, t, :], ps[t][:], ACT.Copy).then_inc(rv_ready, 1)

                def silu_of_g(h):
                    act.wait_ge(slots_used, used(base + 11 + 4 * h))
                    if h:
                        act.wait_ge(gated_ready, 2 * h)
                    for t in range(NT):
                        nc.scalar.activation(silu_g[:, t, :], ps[2 + t][:], ACT.Silu).then_inc(silu_g_ready, 1)

                def gated_hi(h, banks):
                    act.wait_ge(gT_psum, h + 1)
                    for half in range(2):
                        nc.scalar.activation(gT_hi[:, 4 * h + 2 * half:4 * h + 2 * half + 2, :],
                                             banks[half][:].rearrange("p (b q) -> p b q", b=2), ACT.Copy).then_inc(gT_hi_ready, 1)

                for s in (3, 4, 5, 6):
                    split_hi(base + s)
                rqk_copy(0)
                split_hi(base + 7)
                rqk_copy(1)
                split_hi(base + 8)
                split_hi(base + 9)
                rqk_copy(2)
                split_hi(base + 10)
                split_hi(base + 11)
                rqk_copy(3)
                for h in range(RH):
                    split_hi(base + 12 + 4 * h)
                    v_copy(h)
                    split_hi(base + 13 + 4 * h)
                    split_hi(base + 14 + 4 * h)
                    silu_of_g(h)
                    split_hi(base + 15 + 4 * h)
                    gated_hi(h, [ps[4], ps[5]] if h < RH - 1 else [ps[0], ps[1]])
                for s in range(28, RET_SLOTS + 2):
                    split_hi(base + s)
                ending(RET_NORM)

            split_hi(0)
            first_x_hi(0)
            split_hi(1)
            split_hi(2)
            first_x_hi(1)
            ffn(0)
            attention()
            ffn(1)
            ffn(2)
            retention()
            ffn(3)

        @block.vector
        def _(dve):
            def split_lo(s, i=0):
                if s >= N_SLOTS:
                    return
                dve.wait_ge(hi_ready, s + 1 + RING * i)
                nc.vector.tensor_tensor(w_lo[:, s % RING, :], w_raw[:, s % RING, :], w_hi[:, s % RING, :],
                                        ALU.subtract).then_inc(lo_ready, 1)

            def first_x_lo(t):
                for half in range(2):
                    k = slice(4 * half, 4 * half + 4)
                    dve.wait_ge(xhi_ready, 2 * t + half + 1)
                    done = nc.vector.tensor_tensor(xT_lo[:, k, t * P:(t + 1) * P],
                                                   ps[2 * half + t][:].rearrange("p (k q) -> p k q", k=4),
                                                   xT_hi[:, k, t * P:(t + 1) * P], ALU.subtract)
                done.then_inc(xT_ready, 1)

            def norm_stats(norm, t):
                index = NT * norm + t
                if t == 0:
                    dve.wait_ge(y_half_ready, norm + 1)
                else:
                    dve.wait_ge(slots_used, END_SLOT[norm])
                if norm == 0:
                    dve.wait_ge(x_loaded, 32)
                else:
                    dve.wait_ge(xnat_ready, index - 1)
                if norm == ATT_NORM:
                    dve.wait_ge(res_ready, t + 1)
                for n in range(2):
                    half = slice(n * BANK, (n + 1) * BANK)
                    nc.vector.scalar_tensor_tensor(z[:, t, half], x_nat[:, t, half], 1.0 if norm == ATT_NORM else ALPHA,
                                                   Y[t][n][:], ALU.mult, ALU.add).then_inc(sums_ready, 1)
                for n in range(2):
                    dve.wait_ge(sums_ready, 4 * index + n + 1)
                    nc.vector.bn_stats(stats[:, t, n, :], z[:, t, n * BANK:(n + 1) * BANK]).then_inc(sums_ready, 1)
                dve.wait_ge(sums_ready, 4 * index + 4)
                nc.vector.bn_aggr(moments[:, t, :], stats[:, t, :, :].rearrange("p a b -> p (a b)")).then_inc(stats_ready, 1)

            def norm_apply(norm, t):
                index = NT * norm + t
                dve.wait_ge(rstd_ready, index + 1)
                for n in range(2):
                    half = slice(n * BANK, (n + 1) * BANK)
                    nc.vector.tensor_scalar(z[:, t, half], z[:, t, half], moments[:, t, 0:1], rstd[:, t, :],
                                            ALU.subtract, ALU.mult).then_inc(xhat_ready, 1)

            def norm_lo(norm, t):
                number = NT * (norm + 1) + t
                dve.wait_ge(xT_psum, 2 * number + 1)
                dve.wait_ge(consts_loaded, 32)
                dve.wait_ge(xT_ready, number)
                for k in range(4):
                    done = nc.vector.tensor_scalar(xT_full[:, k, :], ps[t][:, k * P:(k + 1) * P],
                                                   cols[:, 0, norm, k:k + 1], cols[:, 1, norm, k:k + 1], ALU.mult, ALU.add)
                done.then_inc(xT_a_full, 1)
                for half in range(2):
                    k = slice(4 * half, 4 * half + 4)
                    dve.wait_ge(xhi_ready, 2 * number + half + 1)
                    done = nc.vector.tensor_tensor(xT_lo[:, k, t * P:(t + 1) * P], xT_full[:, k, :],
                                                   xT_hi[:, k, t * P:(t + 1) * P], ALU.subtract)
                done.then_inc(xT_ready, 1)

            def ending(norm):
                if norm == N_NORMS - 1:
                    return
                norm_stats(norm, 0)
                norm_apply(norm, 0)
                split_lo(END_SLOT[norm] + 2)
                norm_lo(norm, 0)
                norm_stats(norm, 1)
                norm_apply(norm, 1)
                norm_lo(norm, 1)

            def last_norm():
                for t in range(NT):
                    norm_stats(N_NORMS - 1, t)
                    norm_apply(N_NORMS - 1, t)
                    dve.wait_ge(rows_loaded, 32 * N_NORMS)
                    for n in range(2):
                        half = slice(n * BANK, (n + 1) * BANK)
                        dve.wait_ge(xhat_ready, 2 * (NT * (N_NORMS - 1) + t) + n + 1)
                        nc.vector.tensor_tensor(z[:, t, half], z[:, t, half], gain_row[:, half], ALU.mult).then_inc(out_step, 1)
                    for n in range(2):
                        half = slice(n * BANK, (n + 1) * BANK)
                        dve.wait_ge(out_step, 2 * t + n + 1)
                        nc.vector.tensor_tensor(z[:, t, half], z[:, t, half], bias_row[:, half], ALU.add).then_inc(out_ready, 1)

            def ffn(f):
                base = FFN_BASE[f]
                hT_hi, hT_lo, silu_gate, h_nat = ffn_bufs[f]

                def gate(c, i=0):
                    if f or c:
                        dve.wait_ge(hT_psum, NCH * f + c + 2 * i)
                    for t in range(NT):
                        dve.wait_ge(silu_ready, 2 * (NCH * f + c) + t + 1 + 4 * i)
                        nc.vector.scalar_tensor_tensor(h_nat[:, t, :], ps[2 * (c % 2) + t][:, HC:2 * HC], 0.5,
                                                       silu_gate[:, t, :], ALU.mult, ALU.mult).then_inc(h_ready, 1)

                def hidden_lo(c, bank, i=0):
                    dve.wait_ge(hT_hi_ready, NCH * f + c + 1 + 2 * i)
                    at = bass.ds(2 * c + 4 * i, 2) if not isinstance(i, int) else slice(2 * c, 2 * c + 2)
                    nc.vector.tensor_tensor(hT_lo[:, at, :], bank[:].rearrange("p (b q) -> p b q", b=2), hT_hi[:, at, :],
                                            ALU.subtract).then_inc(hT_ready, 1)

                split_lo(base + 3)
                split_lo(base + 4)
                gate(0)
                split_lo(base + 5)
                split_lo(base + 6)
                hidden_lo(0, ps[4])
                with dve.Fori(0, 4) as i:
                    for c in (2, 3):
                        gate(c - 1, i)
                        split_lo(base + 2 * c + 3, i)
                        hidden_lo(c - 1, ps[4 + (c - 1) % 2], i)
                        split_lo(base + 2 * c + 4, i)
                gate(NCH - 2)
                split_lo(base + 2 * NCH + 1)
                hidden_lo(NCH - 2, ps[5])
                split_lo(base + 2 * NCH + 2)
                gate(NCH - 1)
                split_lo(base + 2 * NCH + 3)
                hidden_lo(NCH - 1, ps[0])
                for s in range(2 * NCH + 4, FFN_SLOTS + 2):
                    split_lo(base + s)
                ending(FFN_NORM[f])

            def attention():
                base = ATT_BASE
                step = [0]

                def link(instruction):
                    step[0] += 1
                    instruction.then_inc(soft_step, 1)
                    dve.wait_ge(soft_step, step[0])

                def q_scaled(n):
                    dve.wait_ge(qT_psum, n + 1)
                    for b in range(4):
                        done = nc.vector.tensor_scalar(qT[:, 4 * n + b, :], ps[2 + b // 2][:, (b % 2) * SEQ:(b % 2 + 1) * SEQ],
                                                       bq_col[:, 4 * n + b:4 * n + b + 1], DH ** -0.5, ALU.add, ALU.mult)
                    done.then_inc(qT_ready, 1)

                def peaks(b):
                    bank1, bank0 = ((ps[4], ps[5]), (ps[0], ps[1]))[b % 2]
                    dve.wait_ge(scores_ready, b + 1)
                    if b >= 2:
                        dve.wait_ge(pT_psum, b - 1)
                    p1 = probs[:, b % 2, 0:512].rearrange("p (j k) -> p j k", j=2)
                    p0 = probs[:, b % 2, 512:768].rearrange("p (j k) -> p j k", j=2)
                    nc.vector.tensor_tensor(p1, bank1[:].rearrange("p (j k) -> p j k", j=2),
                                            mask[:, None, :].broadcast_to([P, 2, 2 * P]), ALU.add)
                    nc.vector.tensor_tensor(p0, bank0[:, 0:256].rearrange("p (j k) -> p j k", j=2),
                                            mask[:, None, P:2 * P].broadcast_to([P, 2, P]), ALU.add).then_inc(masked, 1)
                    dve.wait_ge(masked, b + 1)
                    nc.vector.reduce_max(peak[:, b % 2, 0:2], p1, AX.X)
                    link(nc.vector.reduce_max(peak[:, b % 2, 2:4], p0, AX.X))
                    link(nc.vector.tensor_tensor(peak_s[:, b % 2, :], peak[:, b % 2, :], sink[:, b, :], ALU.max))
                    link(nc.vector.tensor_scalar(neg_peak[:, b % 2, :], peak_s[:, b % 2, :], -1.0, None, ALU.mult))
                    nc.vector.tensor_tensor(sink_less[:, b % 2, :], sink[:, b, :], peak_s[:, b % 2, :],
                                            ALU.subtract).then_inc(peaks_ready, 1)

                def normalise(b):
                    dve.wait_ge(exps_ready, b + 1)
                    link(nc.vector.tensor_tensor(total[:, b % 2, :], sums[:, b % 2, :], sink_exp[:, b % 2, :], ALU.add))
                    link(nc.vector.reciprocal(inv[:, b % 2, :], total[:, b % 2, :]))
                    for i, (c, w) in enumerate(((0, 256), (256, 256), (512, P), (640, P))):
                        done = nc.vector.tensor_scalar(probs[:, b % 2, c:c + w], probs[:, b % 2, c:c + w],
                                                       inv[:, b % 2, i:i + 1], None, ALU.mult)
                    done.then_inc(probs_ready, 1)

                def pT0_copy(b):
                    dve.wait_ge(pT_psum, b + 1)
                    if b == 4:
                        dve.wait_ge(o_psum, 1)
                    nc.vector.tensor_copy(pT0[:, :, b % 4, :], ps[3][:, 0:256].rearrange("p (j q) -> p j q", j=2)).then_inc(pT0_ready, 1)

                def o_lo(g):
                    for t in range(NT):
                        dve.wait_ge(oT_hi_ready, 2 * g + t + 1)
                        at = (slice(None), slice(4 * g, 4 * g + 4), slice(t * P, (t + 1) * P))
                        done = nc.vector.tensor_tensor(oT_lo[at], ps[7 - t][:].rearrange("p (b q) -> p b q", b=4),
                                                       oT_hi[at], ALU.subtract)
                    done.then_inc(oT_ready, 1)

                nc.vector.memset(kT[:], 0.0).then_inc(kz_ready, 1)
                split_lo(base + 3)
                dve.wait_ge(att_consts, 16 * 5)
                dve.wait_ge(slots_used, used(base))
                for t in range(NT):
                    for j in range(2):
                        nc.vector.tensor_copy(k_twice[:, t, :, j, :], ps[t][:, 0:P].rearrange("p (g d) -> p g d", g=NKV))
                    nc.vector.tensor_tensor(v_nat[:, t, :], ps[t][:, P:2 * P], bv_row[:], ALU.add).then_inc(kv_nat, 1)
                split_lo(base + 4)
                split_lo(base + 5)
                q_scaled(0)
                split_lo(base + 6)
                for t in range(NT):
                    dve.wait_ge(xnat_ready, t + 1)
                    nc.vector.scalar_tensor_tensor(x_nat[:, t, :], x_nat[:, t, :], ALPHA, bo_row[:], ALU.mult,
                                                   ALU.add).then_inc(res_ready, 1)
                for b in range(NB + 2):
                    if b < NB:
                        peaks(b)
                    if b == 1:
                        q_scaled(1)
                    if b >= 1 and b <= NB:
                        normalise(b - 1)
                    if b >= 2:
                        pT0_copy(b - 2)
                    if b == 3:
                        split_lo(base + 7)
                    if b == 5:
                        split_lo(base + 8)
                    if b == 7:
                        o_lo(0)
                o_lo(1)
                split_lo(base + 9)
                split_lo(base + 10)
                ending(ATT_NORM)

            def retention():
                base = RET_BASE
                step = [0]

                def turn(c):
                    dve.wait_ge(slots_used, used(base + 2 * c + 1))
                    if c:
                        dve.wait_ge(rqkT_psum, c)
                    for t in range(NT):
                        halves = ps[2 * (c % 2) + t][:].rearrange("p (h f) -> p h f", f=P)
                        cos, sin = (rope[:, t, j:j + 1, :].broadcast_to([P, 4, P]) for j in range(2))
                        if c or t:
                            dve.wait_ge(rot_ready, 2 * c + t)
                        nc.vector.tensor_tensor(by_cos[:].rearrange("p (h f) -> p h f", f=P), halves, cos, ALU.mult)
                        nc.vector.tensor_tensor(by_sin[:].rearrange("p (h f) -> p h f", f=P), halves, sin,
                                                ALU.mult).then_inc(rot_step, 1)
                        c4, s4, r4 = (a.rearrange("p (h e f) -> p h e f", h=2, e=2) for a in (by_cos[:], by_sin[:], rot[:, t, :]))
                        dve.wait_ge(rot_step, step[0] + 1)
                        nc.vector.tensor_tensor(r4[:, :, 0, :], c4[:, :, 0, :], s4[:, :, 1, :], ALU.subtract).then_inc(rot_step, 1)
                        nc.vector.tensor_tensor(r4[:, :, 1, :], s4[:, :, 0, :], c4[:, :, 1, :], ALU.add).then_inc(rot_ready, 1)
                        step[0] += 2

                def decayed(h):
                    dve.wait_ge(scT_psum, h + 1)
                    nc.vector.tensor_tensor(scT[:, h, :], ps[6 + h % 2][:, 0:384], decay[:, h, :], ALU.mult).then_inc(scT_ready, 1)

                def group_stats(h):
                    dve.wait_ge(ry_psum, h + 1)
                    for t in range(NT):
                        nc.vector.bn_stats(gn_stats[:, t, :], ps[6 + t][:]).then_inc(gn_step, 1)
                    for t in range(NT):
                        dve.wait_ge(gn_step, 2 * h + t + 1)
                        nc.vector.bn_aggr(gn_moments[:, t, :], gn_stats[:, t, :]).then_inc(gn_stats_ready, 1)

                def group_norm(h):
                    dve.wait_ge(gn_rstd_ready, 2 * h + 2)
                    if h:
                        dve.wait_ge(gT_psum, h)
                    for t in range(NT):
                        nc.vector.tensor_scalar(y_nat[:, t, :], ps[6 + t][:], gn_moments[:, t, 0:1], gn_rstd[:, t, :],
                                                ALU.subtract, ALU.mult).then_inc(yn_ready, 1)

                def gated(h):
                    for t in range(NT):
                        dve.wait_ge(silu_g_ready, 2 * h + t + 1)
                        dve.wait_ge(yn_ready, 2 * h + t + 1)
                        nc.vector.tensor_tensor(y_nat[:, t, :], y_nat[:, t, :], silu_g[:, t, :], ALU.mult).then_inc(gated_ready, 1)

                def gated_lo(h, banks):
                    for half in range(2):
                        dve.wait_ge(gT_hi_ready, 2 * h + half + 1)
                        at = slice(4 * h + 2 * half, 4 * h + 2 * half + 2)
                        done = nc.vector.tensor_tensor(gT_lo[:, at, :], banks[half][:].rearrange("p (b q) -> p b q", b=2),
                                                       gT_hi[:, at, :], ALU.subtract)
                    done.then_inc(gT_ready, 1)

                dve.wait_ge(ret_consts, 32)
                split_lo(base + 3)
                split_lo(base + 4)
                turn(0)
                split_lo(base + 5)
                split_lo(base + 6)
                turn(1)
                split_lo(base + 7)
                split_lo(base + 8)
                turn(2)
                split_lo(base + 9)
                split_lo(base + 10)
                turn(3)
                split_lo(base + 11)
                for h in range(RH):
                    split_lo(base + 12 + 4 * h)
                    if h == 0:
                        for head in range(RH):
                            decayed(head)
                    split_lo(base + 13 + 4 * h)
                    group_stats(h)
                    group_norm(h)
                    split_lo(base + 14 + 4 * h)
                    gated(h)
                    split_lo(base + 15 + 4 * h)
                    gated_lo(h, [ps[4], ps[5]] if h < RH - 1 else [ps[0], ps[1]])
                for s in range(28, RET_SLOTS + 2):
                    split_lo(base + s)
                ending(RET_NORM)

            split_lo(0)
            first_x_lo(0)
            split_lo(1)
            split_lo(2)
            first_x_lo(1)
            ffn(0)
            attention()
            ffn(1)
            ffn(2)
            retention()
            ffn(3)
            last_norm()

        @block.gpsimd
        def _(pool):
            def rows_for(norm):
                for j, row in enumerate((gain_row, bias_row)):
                    pool.dma_start(row[:], norm_rows[j, norm:norm + 1, :].broadcast_to([P, D])).then_inc(rows_loaded, 16)

            def reciprocal_roots(norm):
                for t in range(NT):
                    index = NT * norm + t
                    pool.wait_ge(stats_ready, index + 1)
                    nc.gpsimd.tensor_tensor(rstd[:, t, :], moments[:, t, 1:2], eps_pow[:, 0:1], ALU.add).then_inc(var_ready, 1)
                    pool.wait_ge(var_ready, index + 1)
                    nc.gpsimd.tensor_tensor(rstd[:, t, :], rstd[:, t, :], eps_pow[:, 2:3], ALU.pow).then_inc(rstd_ready, 1)

            def residual(norm):
                pool.wait_ge(rows_loaded, 32 * (norm + 1))
                for t in range(NT):
                    index = NT * norm + t
                    pool.wait_ge(xhat_ready, 2 * index + 2)
                    nc.gpsimd.tensor_tensor(x_nat[:, t, :], z[:, t, :], gain_row[:], ALU.mult).then_inc(x_scaled, 1)
                    pool.wait_ge(x_scaled, index + 1)
                    nc.gpsimd.tensor_tensor(x_nat[:, t, :], x_nat[:, t, :], bias_row[:], ALU.add).then_inc(xnat_ready, 1)

            def norm_of(norm):
                reciprocal_roots(norm)
                if norm < N_NORMS - 1:
                    residual(norm)
                    pool.wait_ge(xnat_ready, NT * (norm + 1))
                    rows_for(norm + 1)

            nc.gpsimd.memset(eps_pow[:, 0:1], LN_EPS)
            nc.gpsimd.memset(eps_pow[:, 1:2], GN_EPS)
            nc.gpsimd.memset(eps_pow[:, 2:3], -0.5).then_inc(eps_ready, 1)
            pool.wait_ge(eps_ready, 1)
            rows_for(0)
            norm_of(0)
            pool.wait_ge(slots_used, END_SLOT[0])
            pool.dma_start(mask[:], mask_in).then_inc(att_consts, 16)
            pool.dma_start(bq_col[:], att_cols).then_inc(att_consts, 16)
            pool.dma_start(sink[:], sinks).then_inc(att_consts, 16)
            pool.dma_start(bo_row[:], att_rows[0:1, 0:D].broadcast_to([P, D])).then_inc(att_consts, 16)
            pool.dma_start(bv_row[:], att_rows[0:1, D:D + NKV * DH].broadcast_to([P, NKV * DH])).then_inc(att_consts, 16)
            for norm in (1, 2, 3):
                norm_of(norm)
            pool.wait_ge(slots_used, END_SLOT[3])
            pool.dma_start(rope[:], rope_in).then_inc(ret_consts, 16)
            pool.dma_start(decay[:], decay_in).then_inc(ret_consts, 16)
            for h in range(RH):
                for t in range(NT):
                    index = NT * h + t
                    pool.wait_ge(gn_stats_ready, index + 1)
                    nc.gpsimd.tensor_tensor(gn_rstd[:, t, :], gn_moments[:, t, 1:2], eps_pow[:, 1:2], ALU.add).then_inc(gn_var, 1)
                    pool.wait_ge(gn_var, index + 1)
                    nc.gpsimd.tensor_tensor(gn_rstd[:, t, :], gn_rstd[:, t, :], eps_pow[:, 2:3], ALU.pow).then_inc(gn_rstd_ready, 1)
            for norm in (4, 5):
                norm_of(norm)


def pack_slots(w, columns):
    import numpy as np
    k = w.shape[0] // P
    blocks = w.reshape(k, P, -1)[:, :, columns]
    per_slot = SLOT // len(columns)
    assert k % per_slot == 0
    return np.transpose(blocks.reshape(k // per_slot, per_slot, P, len(columns)), (0, 2, 1, 3)).reshape(-1, P, SLOT)


def kernel(x, ln_g, ln_b, ffn1_w_gate_up, ffn1_w_down, ffn2_w_gate_up, ffn2_w_down,
           attn_w_qkv, attn_b_qkv, attn_sinks, attn_w_o, attn_b_o, ret_w_qkvg, ret_w_o):
    import numpy as np
    import concourse.bacc as bacc
    from concourse.bass_utils import run_bass_kernel_spmd

    slots = []

    def add_ffn(w_gate_up, w_down):
        for c in range(NCH):
            at = np.arange(c * HC, (c + 1) * HC)
            slots.append(pack_slots(w_gate_up, np.concatenate([at, FFN + at])))
        slots.append(pack_slots(w_down, np.arange(D)))

    add_ffn(ffn1_w_gate_up[0], ffn1_w_down[0])
    slots.append(pack_slots(attn_w_qkv[0], np.arange(D, D + 256)))
    for n in range(2):
        slots.append(pack_slots(attn_w_qkv[0], np.arange(n * BANK, (n + 1) * BANK)))
    slots.append(pack_slots(attn_w_o[0], np.arange(D)))
    add_ffn(ffn2_w_gate_up[0], ffn2_w_down[0])
    add_ffn(ffn1_w_gate_up[1], ffn1_w_down[1])
    order = [0, 1, 2, 3] + [c for h in range(RH) for c in (4 + h, 8 + h)]
    for c in order:
        slots.append(pack_slots(ret_w_qkvg[0], np.arange(c * BANK, (c + 1) * BANK)))
    slots.append(pack_slots(ret_w_o[0], np.arange(D)))
    add_ffn(ffn2_w_gate_up[1], ffn2_w_down[1])
    weights = np.concatenate(slots).reshape(-1, SLOT)
    assert weights.shape[0] == N_SLOTS * P

    norm_rows = np.stack([ln_g.reshape(N_NORMS, D), ln_b.reshape(N_NORMS, D)])
    norm_cols = np.transpose(norm_rows.reshape(2, N_NORMS, KD, P), (3, 0, 1, 2))
    b = attn_b_qkv[0]
    bias_q = b[:D].reshape(NB, P)
    bias_k = b[D:D + NKV * DH].reshape(NKV, 1, DH)
    att_cols = np.concatenate([bias_q, np.repeat(bias_k, 2, axis=1).reshape(NKV, P)]).T
    pairs = attn_sinks[0].reshape(NB, 2)
    sinks = np.broadcast_to(np.concatenate([pairs, pairs], axis=1)[None], (P, NB, 4))
    att_rows = np.concatenate([attn_b_o[0], b[D + NKV * DH:]])[None]

    f = np.float32
    key, query = np.arange(P)[:, None], np.arange(P)[None, :]
    ident = np.eye(P, dtype=f)
    mask = np.concatenate([np.where(query > key, 0.0, -1e30), np.where(query <= key, 0.0, -1e30)], axis=1).astype(f)
    freqs = (f(1.0) / (f(10000.0) ** np.linspace(0.0, 1.0, P, dtype=f))).astype(f)
    angle = (np.arange(SEQ, dtype=f)[:, None] * freqs[None, :]).astype(np.float64)
    rope = np.stack([np.cos(angle), np.sin(angle)], axis=1).astype(f).reshape(NT, P, 2, P).transpose(1, 0, 2, 3)
    gamma = 1.0 - 2.0 ** (-5.0 - np.arange(RH))
    ahead = np.concatenate([query - key, query + P - key, query - key], axis=1)
    decay = np.where(ahead >= 0, gamma[:, None, None] ** np.maximum(ahead, 0), 0.0) * RQ ** -0.5
    decay = decay.transpose(1, 0, 2).astype(f)

    arrays = {"x": x.reshape(SEQ, D), "weights": weights, "norm_rows": norm_rows, "norm_cols": norm_cols,
              "att_cols": att_cols, "sinks": sinks, "att_rows": att_rows, "ident_in": ident, "mask_in": mask,
              "rope_in": rope, "decay_in": decay}
    arrays = {n: np.ascontiguousarray(a) for n, a in arrays.items()}
    nc = bacc.Bacc("TRN2", target_bir_lowering=False, num_devices=1)
    f32 = mybir.dt.float32
    handles = {n: nc.dram_tensor(n, a.shape, f32, kind="ExternalInput").ap() for n, a in arrays.items()}
    out = nc.dram_tensor("out", (SEQ, D), f32, kind="ExternalOutput").ap()
    trunk(nc, out=out, **handles)
    result = run_bass_kernel_spmd(nc, [arrays], core_ids=[0])
    return result.results[0]["out"].reshape(1, SEQ, D)
```

```python
import concourse.bass as bass
from concourse import mybir
from contextlib import ExitStack

P = 128
D = 1024
SEQ = 256
NT = SEQ // P
KD = D // P
FFN = 2816
HC = 256
NCH = FFN // HC
KF = FFN // P
NH, NKV, DH = 16, 2, 64
NB = NH // 2
RH, RQ, RV = 4, 256, 512
SLOT = 2048
RING = 4
BANK = 512
ALPHA = (2.0 * 2) ** 0.25
LN_EPS, GN_EPS = 1e-5, 1e-6

FFN_SLOTS = 2 * NCH + KF // 2
ATT_SLOTS = 1 + 4 + 4
RET_SLOTS = 24 + 8
FFN_BASE = [0, FFN_SLOTS + ATT_SLOTS, 2 * FFN_SLOTS + ATT_SLOTS, 3 * FFN_SLOTS + ATT_SLOTS + RET_SLOTS]
ATT_BASE = FFN_SLOTS
RET_BASE = 3 * FFN_SLOTS + ATT_SLOTS
N_SLOTS = 4 * FFN_SLOTS + ATT_SLOTS + RET_SLOTS
FFN_NORM = [0, 2, 3, 5]
ATT_NORM, RET_NORM = 1, 4
N_NORMS = 6
END_SLOT = [FFN_SLOTS, ATT_BASE + ATT_SLOTS, FFN_BASE[1] + FFN_SLOTS, FFN_BASE[2] + FFN_SLOTS,
            RET_BASE + RET_SLOTS, N_SLOTS]


def trunk(nc, x, weights, norm_rows, norm_cols, att_cols, sinks, att_rows, ident_in, mask_in, rope_in, decay_in, out):
    f32 = mybir.dt.float32
    f32r = mybir.dt.float32r
    ALU = mybir.AluOpType
    ACT = mybir.ActivationFunctionType
    AX = mybir.AxisListType

    ctx = ExitStack()
    with ctx:
        def sb(name, shape, dt=f32, within=ctx):
            return within.enter_context(nc.sbuf_tensor(name, shape, dt))

        def sem(name):
            return ctx.enter_context(nc.semaphore(name))

        w_raw = sb("w_raw", [P, RING, SLOT])
        w_hi = sb("w_hi", [P, RING, SLOT], f32r)
        w_lo = sb("w_lo", [P, RING, SLOT], f32r)
        xT_hi = sb("xT_hi", [P, KD, SEQ], f32r)
        xT_lo = sb("xT_lo", [P, KD, SEQ], f32r)
        x_nat = sb("x_nat", [P, NT, D])
        z = sb("z", [P, NT, D])
        xT_full = sb("xT_full", [P, KD, P])
        gain_row = sb("gain_row", [P, D])
        bias_row = sb("bias_row", [P, D])
        cols = sb("cols", [P, 2, N_NORMS, KD])
        stats = sb("stats", [P, NT, 2, 6])
        moments = sb("moments", [P, NT, 2])
        rstd = sb("rstd", [P, NT, 1])
        eps_pow = sb("eps_pow", [P, 3])
        ident = sb("ident", [P, P])
        gn_stats = sb("gn_stats", [P, NT, 6])
        gn_moments = sb("gn_moments", [P, NT, 2])
        gn_rstd = sb("gn_rstd", [P, NT, 1])

        def ffn_tensors(f):
            with ExitStack() as r:
                return [sb(f"{n}{f}", s, d, r) for n, s, d in (
                    ("hT_hi", [P, KF, SEQ], f32r), ("hT_lo", [P, KF, SEQ], f32r),
                    ("silu_gate", [P, NT, HC], f32), ("h_nat", [P, NT, HC], f32))]

        ffn_bufs = [ffn_tensors(f) for f in range(4)]
        with ExitStack() as r:
            oT_hi = sb("oT_hi", [P, NB, SEQ], f32r, r)
            oT_lo = sb("oT_lo", [P, NB, SEQ], f32r, r)
            q_nat = sb("q_nat", [P, NT, BANK], f32, r)
            qT = sb("qT", [P, NB, SEQ], f32, r)
            k_twice = sb("k_twice", [P, NT, NKV, 2, DH], f32, r)
            kT = sb("kT", [P, NKV, 2, SEQ], f32, r)
            v_nat = sb("v_nat", [P, NT, NKV * DH], f32, r)
            probs = sb("probs", [P, 4, 768], f32, r)
            pT1 = sb("pT1", [P, 2, 2, 4, P], f32, r)
            pT0 = sb("pT0", [P, 2, 4, P], f32, r)
            mask = sb("mask", [P, 2 * P], f32, r)
            bo_row = sb("bo_row", [P, D], f32, r)
            bv_row = sb("bv_row", [P, NKV * DH], f32, r)
            bq_col = sb("bq_col", [P, NB + NKV], f32, r)
            sink = sb("sink", [P, NB, 4], f32, r)
            neg_sink = sb("neg_sink", [P, NB, 4], f32, r)
            neg_peak = sb("neg_peak", [P, 4, 4], f32, r)
            sink_less = sb("sink_less", [P, 4, 4], f32, r)
            sink_exp = sb("sink_exp", [P, 4, 4], f32, r)
            sums = sb("sums", [P, 4, 4], f32, r)
            total = sb("total", [P, 4, 4], f32, r)
            inv = sb("inv", [P, 4, 4], f32, r)
        with ExitStack() as r:
            scT = sb("scT", [P, RH, 384], f32, r)
            rv = sb("rv", [P, NT, RV], f32, r)
            silu_g = sb("silu_g", [P, NT, RV], f32, r)
            y_nat = sb("y_nat", [P, NT, RV], f32, r)
            decay = sb("decay", [P, RH, 384], f32, r)
            rope = sb("rope", [P, NT, 2, P], f32, r)
            with ExitStack() as early:
                rqkT = sb("rqkT", [P, 16, SEQ], f32, early)
                by_cos = sb("by_cos", [P, BANK], f32, early)
                by_sin = sb("by_sin", [P, BANK], f32, early)
                rot = sb("rot", [P, NT, BANK], f32, early)
            gT_hi = sb("gT_hi", [P, 16, SEQ], f32r, r)
            gT_lo = sb("gT_lo", [P, 16, SEQ], f32r, r)

        ps = [ctx.enter_context(nc.psum_tensor(f"bank{b}", [P, BANK], f32)) for b in range(8)]
        O = [[ps[7], ps[6]], [ps[1], ps[0]]]
        Y = [[ps[4 + 2 * t + n] for n in range(2)] for t in range(NT)]

        first_raw = [sem(f"first_raw{i}") for i in range(3)]
        first_hi = sem("first_hi")
        first_lo = sem("first_lo")
        raw_loaded = [sem(f"raw_loaded{i}") for i in range(RING)]
        x_loaded = [sem(f"x_loaded{t}") for t in range(NT)]
        ident_loaded = sem("ident_loaded")
        cols_loaded = sem("cols_loaded")
        rows_loaded = sem("rows_loaded")
        att_consts = sem("att_consts")
        ret_consts = sem("ret_consts")
        hi_ready = sem("hi_ready")
        lo_ready = sem("lo_ready")
        slots_used = sem("slots_used")
        y_ready = sem("y_ready")
        sums_ready = sem("sums_ready")
        stats_ready = sem("stats_ready")
        var_ready = sem("var_ready")
        rstd_ready = sem("rstd_ready")
        xhat_ready = sem("xhat_ready")
        xT_psum = sem("xT_psum")
        xT_a_full = sem("xT_a_full")
        xT_a_hi = sem("xT_a_hi")
        xT_b_full = sem("xT_b_full")
        xT_b_hi = sem("xT_b_hi")
        xT_ready = sem("xT_ready")
        x_scaled = sem("x_scaled")
        xnat_ready = sem("xnat_ready")
        res_ready = sem("res_ready")
        eps_ready = sem("eps_ready")
        silu_ready = sem("silu_ready")
        h_ready = sem("h_ready")
        hT_psum = sem("hT_psum")
        hT_hi_ready = sem("hT_hi_ready")
        hT_ready = sem("hT_ready")
        kz_ready = sem("kz_ready")
        kv_nat = sem("kv_nat")
        kT_psum = sem("kT_psum")
        kT_ready = sem("kT_ready")
        q_nat_ready = sem("q_nat_ready")
        qT_psum = sem("qT_psum")
        qT_ready = sem("qT_ready")
        scores_ready = sem("scores_ready")
        soft_step = sem("soft_step")
        peaks_ready = sem("peaks_ready")
        exps_ready = sem("exps_ready")
        inv_ready = sem("inv_ready")
        probs_ready = sem("probs_ready")
        pT_psum = sem("pT_psum")
        pT1_ready = sem("pT1_ready")
        pT0_ready = sem("pT0_ready")
        o_psum = sem("o_psum")
        oT_hi_ready = sem("oT_hi_ready")
        oT_ready = sem("oT_ready")
        rot_step = sem("rot_step")
        rot_ready = sem("rot_ready")
        rqkT_psum = sem("rqkT_psum")
        rqkT_ready = sem("rqkT_ready")
        scT_psum = sem("scT_psum")
        scT_ready = sem("scT_ready")
        rv_ready = sem("rv_ready")
        ry_psum = sem("ry_psum")
        gn_step = sem("gn_step")
        gn_stats_ready = sem("gn_stats_ready")
        gn_var = sem("gn_var")
        gn_rstd_ready = sem("gn_rstd_ready")
        yn_ready = sem("yn_ready")
        silu_g_ready = sem("silu_g_ready")
        gated_ready = sem("gated_ready")
        gT_psum = sem("gT_psum")
        gT_hi_ready = sem("gT_hi_ready")
        gT_ready = sem("gT_ready")
        out_step = sem("out_step")
        out_ready = sem("out_ready")
        out_stored = sem("out_stored")

        def used(s):
            return s + 1

        block = ctx.enter_context(nc.Block())

        @block.sync
        def _(sp):
            def load(s, i=0):
                if s >= RING:
                    sp.wait_ge(lo_ready, s - RING + 1 + RING * i)
                sp.dma_start(w_raw[:, s % RING, :], weights[bass.ds((s + RING * i) * P, P), :]).then_inc(raw_loaded[s % RING], 16)

            for k in range(4):
                at = slice(k * BANK, (k + 1) * BANK)
                sp.dma_start(w_raw[:, 0, at], weights[0:P, at]).then_inc(first_raw[k] if k < 3 else raw_loaded[0], 16)
            for s in range(1, RING):
                load(s)
            sp.dma_start(cols[:], norm_cols).then_inc(cols_loaded, 16)
            with sp.Fori(0, N_SLOTS // RING - 1) as i:
                for s in range(RING, 2 * RING):
                    load(s, i)
            for s in range(N_SLOTS // RING * RING, N_SLOTS):
                load(s)
            for t in range(NT):
                for n in range(2):
                    sp.wait_ge(out_ready, 2 * t + n + 1)
                    sp.dma_start(out[t * P:(t + 1) * P, n * BANK:(n + 1) * BANK],
                                 z[:, t, n * BANK:(n + 1) * BANK]).then_inc(out_stored, 16)
            sp.wait_ge(out_stored, 16 * 2 * NT)

        @block.tensor
        def _(pe):
            def three(bank, hi, lo, whi, wlo, start, stop):
                nc.tensor.matmul(bank, hi, whi, start=start, stop=False)
                nc.tensor.matmul(bank, hi, wlo, start=False, stop=False)
                return nc.tensor.matmul(bank, lo, whi, start=False, stop=stop)

            def part(s, t, width, act_hi, act_lo, k, at, banks, start, stop, halves=None):
                tok = slice(t * P, (t + 1) * P)
                for n in halves or range(len(banks)):
                    w = slice(at * width + n * BANK, at * width + min(width, (n + 1) * BANK))
                    done = three(banks[n][:, 0:min(width, BANK)], act_hi[:, k, tok], act_lo[:, k, tok],
                                 w_hi[:, s % RING, w], w_lo[:, s % RING, w], start, stop)
                return done

            def wait_slot(s, i=0):
                pe.wait_ge(lo_ready, s + 1 + RING * i)

            def x_transposes(number, t, src):
                for half in range(2):
                    if number >= NT:
                        pe.wait_ge(xhat_ready, 2 * (number - NT) + half + 1)
                    for k in range(4):
                        f = slice((4 * half + k) * P, (4 * half + k + 1) * P)
                        done = nc.tensor.transpose(ps[2 * half + t][:, k * P:(k + 1) * P], src[:, t, f], ident[:])
                    done.then_inc(xT_psum, 1)

            def norm_number(norm, t):
                return NT * (norm + 1) + t

            def opening(base, spec, norm):
                for t in range(NT):
                    number = norm_number(norm, t)
                    for j, (width, banks, parts) in enumerate(spec):
                        if t == 0 and j == 2:
                            if norm < 0:
                                pe.wait_ge(x_loaded[1], 16)
                            x_transposes(norm_number(norm, 1), 1, x_nat if norm < 0 else z)
                        if t == 0 and base + j > 0:
                            wait_slot(base + j)
                        for k0, first, last in parts:
                            if (j, k0) in ((0, 0), (0, 4), (1, 4)):
                                pe.wait_ge(xT_ready, 2 * number + 1 + k0 // 4)
                            for k in range(4):
                                if t == 0 and base + j == 0:
                                    pe.wait_ge(*((first_lo, k + 1) if k < 3 else (lo_ready, 1)))
                                done = part(base + j, t, width, xT_hi, xT_lo, k0 + k, k0 + k - parts[0][0], [banks[t]],
                                            first and k == 0, last and k == 3)
                        if t == 1:
                            done.then_inc(slots_used, 1)

            def closing(base, act_hi, act_lo, k0, norm, parted=None):
                for t in range(NT):
                    if parted:
                        pe.wait_ge(oT_ready, parted + t + 1)
                    for n in range(2):
                        for j in range(2):
                            if t == 0 and n == 0:
                                wait_slot(base + j)
                            if t == 1 and n == 1 and j == 1 and norm < N_NORMS - 1:
                                x_transposes(norm_number(norm, 0), 0, z)
                            for k in range(2):
                                done = part(base + j, t, D, act_hi, act_lo, k0 + 2 * j + k, k, Y[t], False,
                                            j == 1 and k == 1, halves=(n,))
                            if t == 1 and n == 1:
                                done.then_inc(slots_used, 1)
                        if (t, n) != (1, 1):
                            done.then_inc(y_ready, 1)

            def output_slot(s, act_hi, act_lo, k0, first, between=None):
                wait_slot(s)
                for t in range(NT):
                    if t and between:
                        between()
                    for k in range(2):
                        done = part(s, t, D, act_hi, act_lo, k0 + k, k, Y[t], first and k == 0, False)
                done.then_inc(slots_used, 1)

            def half_chunk(s, half, banks, i=0, between=None):
                wait_slot(s, i)
                for t in range(NT):
                    if t and between:
                        between()
                    for k in range(4):
                        done = part(s, t, BANK, xT_hi, xT_lo, 4 * half + k, k, [banks[t]],
                                    half == 0 and k == 0, half == 1 and k == 3)
                done.then_inc(slots_used, 1)

            def ffn(f):
                base = FFN_BASE[f]
                hT_hi, hT_lo, _, h_nat = ffn_bufs[f]
                pair = [[ps[0], ps[1]], [ps[2], ps[3]]]

                def h_transposes(c, bank, i=0):
                    pe.wait_ge(h_ready, 2 * (NCH * f + c) + 2 + 4 * i)
                    for b in range(2):
                        for t in range(NT):
                            done = nc.tensor.transpose(bank[:, (2 * b + t) * P:(2 * b + t + 1) * P],
                                                       h_nat[:, t, b * P:(b + 1) * P], ident[:])
                    done.then_inc(hT_psum, 1)

                opening(base, [(BANK, pair[0], [(0, True, False)]), (BANK, pair[0], [(4, False, True)]),
                               (BANK, pair[1], [(0, True, False)])], FFN_NORM[f] - 1)
                half_chunk(base + 3, 1, pair[1])
                h_transposes(0, ps[4])
                with pe.Fori(0, 4) as i:
                    for c in (2, 3):
                        pe.wait_ge(h_ready, 2 * (NCH * f + c - 2) + 2 + 4 * i)
                        half_chunk(base + 2 * c, 0, pair[c % 2], i)
                        h_transposes(c - 1, ps[4 + (c - 1) % 2], i)
                        half_chunk(base + 2 * c + 1, 1, pair[c % 2], i)
                pe.wait_ge(h_ready, 2 * (NCH * f + NCH - 3) + 2)
                half_chunk(base + 2 * NCH - 2, 0, pair[0])
                h_transposes(NCH - 2, ps[5])
                half_chunk(base + 2 * NCH - 1, 1, pair[0])
                down = base + 2 * NCH
                for d in range(NCH - 2):
                    pe.wait_ge(hT_ready, NCH * f + NCH - 1)
                    output_slot(down + d, hT_hi, hT_lo, 2 * d, d == 0)
                    if d == 0:
                        h_transposes(NCH - 1, ps[0])
                pe.wait_ge(hT_ready, NCH * f + NCH)
                closing(down + NCH - 2, hT_hi, hT_lo, 2 * (NCH - 2), FFN_NORM[f])

            def attention():
                base = ATT_BASE
                opening(base, [(256, [ps[0], ps[1]], [(0, True, False), (4, False, True)]),
                               (BANK, [ps[2], ps[3]], [(0, True, False)]),
                               (BANK, [ps[2], ps[3]], [(4, False, True)])], ATT_NORM - 1)

                def k_transposes():
                    pe.wait_ge(kv_nat, NT)
                    for g in range(NKV):
                        for t in range(NT):
                            done = nc.tensor.transpose(ps[0][:, (2 * g + t) * P:(2 * g + t + 1) * P],
                                                       k_twice[:, t, g, :, :].rearrange("p a b -> p (a b)"), ident[:])
                    done.then_inc(kT_psum, 1)

                def q_transposes(n):
                    pe.wait_ge(q_nat_ready, n + 1)
                    for b in range(4):
                        for t in range(NT):
                            c = (2 * (b % 2) + t) * P
                            done = nc.tensor.transpose(ps[(2, 6)[n] + b // 2][:, c:c + P], q_nat[:, t, b * P:(b + 1) * P], ident[:])
                    done.then_inc(qT_psum, 1)

                def scores(b):
                    bank1, bank0 = ((ps[4], ps[5]), (ps[0], ps[1]))[b % 2]
                    if b == 0:
                        pe.wait_ge(kT_ready, 1)
                    if b % 4 == 0:
                        pe.wait_ge(qT_ready, b // 4 + 1)
                    if b >= 2:
                        pe.wait_ge(peaks_ready, b - 1)
                    g = b // 4
                    nc.tensor.matmul(bank1[:], qT[:, b, P:2 * P], kT[:, g, :, :].rearrange("p j k -> p (j k)"),
                                     start=True, stop=True)
                    nc.tensor.matmul(bank0[:, 0:2 * P], qT[:, b, 0:P], kT[:, g, :, 0:P],
                                     start=True, stop=True).then_inc(scores_ready, 1)

                def p_transposes(b):
                    pe.wait_ge(probs_ready, b + 1)
                    if b == 0:
                        pe.wait_ge(qT_ready, 1)
                    else:
                        pe.wait_ge(pT1_ready, b)
                        pe.wait_ge(pT0_ready, b)
                    for j in range(2):
                        for kb in range(2):
                            nc.tensor.transpose(ps[2][:, (2 * j + kb) * P:(2 * j + kb + 1) * P],
                                                probs[:, b % 4, j * 256 + kb * P:j * 256 + (kb + 1) * P], ident[:])
                    for j in range(2):
                        done = nc.tensor.transpose(ps[3][:, j * P:(j + 1) * P],
                                                   probs[:, b % 4, 512 + j * P:512 + (j + 1) * P], ident[:])
                    done.then_inc(pT_psum, 1)

                def values(g):
                    pe.wait_ge(pT1_ready, 4 * g + 4)
                    pe.wait_ge(pT0_ready, 4 * g + 4)
                    if g:
                        pe.wait_ge(peaks_ready, NB)
                    v = [v_nat[:, t, g * DH:(g + 1) * DH] for t in range(NT)]
                    o0, o1 = O[g]
                    for j in range(2):
                        done = nc.tensor.matmul(o0[j * DH:(j + 1) * DH, :], v[0], pT0[:, j, :, :].rearrange("p b q -> p (b q)"),
                                                start=True, stop=True)
                    done.then_inc(o_psum, 1)
                    for j in range(2):
                        for kb in range(2):
                            done = nc.tensor.matmul(o1[j * DH:(j + 1) * DH, :], v[kb],
                                                    pT1[:, kb, j, :, :].rearrange("p b q -> p (b q)"), start=kb == 0, stop=kb == 1)
                    done.then_inc(o_psum, 1)

                half_chunk(base + 3, 0, [ps[6], ps[7]], between=lambda: (k_transposes(), q_transposes(0)))
                scores(0)
                scores(1)
                half_chunk(base + 4, 1, [ps[6], ps[7]])
                scores(2)
                q_transposes(1)
                scores(3)
                for b in range(4):
                    p_transposes(b)
                    scores(b + 4)
                values(0)
                p_transposes(4)
                p_transposes(5)
                pe.wait_ge(oT_ready, 2)
                pe.wait_ge(peaks_ready, NB)
                output_slot(base + 5, oT_hi, oT_lo, 0, True, between=lambda: p_transposes(6))
                output_slot(base + 6, oT_hi, oT_lo, 2, False, between=lambda: p_transposes(7))
                values(1)
                closing(base + 7, oT_hi, oT_lo, 4, ATT_NORM, parted=2)

            def retention():
                base = RET_BASE
                pair = [[ps[0], ps[1]], [ps[2], ps[3]]]

                def rot_transposes(c):
                    pe.wait_ge(rot_ready, 2 * c + 2)
                    if c:
                        pe.wait_ge(rqkT_ready, c)
                    for b in range(4):
                        for t in range(NT):
                            col = (2 * (b % 2) + t) * P
                            done = nc.tensor.transpose(ps[4 + b // 2][:, col:col + P], rot[:, t, b * P:(b + 1) * P], ident[:])
                    done.then_inc(rqkT_psum, 1)

                def ret_scores(h):
                    bank = ps[6 + h % 2]
                    if h >= 2:
                        pe.wait_ge(scT_ready, h - 1)
                    for half in range(2):
                        nc.tensor.matmul(bank[:, 0:256], rqkT[:, 8 + 2 * h + half, 0:P], rqkT[:, 2 * h + half, :],
                                         start=half == 0, stop=half == 1)
                    for half in range(2):
                        done = nc.tensor.matmul(bank[:, 256:384], rqkT[:, 8 + 2 * h + half, P:SEQ],
                                                rqkT[:, 2 * h + half, P:SEQ], start=half == 0, stop=half == 1)
                    done.then_inc(scT_psum, 1)

                def ret_values(h):
                    pe.wait_ge(scT_ready, RH)
                    pe.wait_ge(rv_ready, 2 * h + 2)
                    if h:
                        pe.wait_ge(yn_ready, 2 * h)
                    nc.tensor.matmul(ps[6][:], scT[:, h, 0:P], rv[:, 0, :], start=True, stop=True)
                    nc.tensor.matmul(ps[7][:], scT[:, h, P:2 * P], rv[:, 0, :], start=True, stop=False)
                    nc.tensor.matmul(ps[7][:], scT[:, h, 2 * P:3 * P], rv[:, 1, :], start=False, stop=True).then_inc(ry_psum, 1)

                def gated_transposes(h, banks):
                    pe.wait_ge(gated_ready, 2 * h + 2)
                    if h:
                        pe.wait_ge(gT_ready, h)
                    for b in range(4):
                        for t in range(NT):
                            col = (2 * (b % 2) + t) * P
                            done = nc.tensor.transpose(banks[b // 2][:, col:col + P], y_nat[:, t, b * P:(b + 1) * P], ident[:])
                    done.then_inc(gT_psum, 1)

                opening(base, [(BANK, pair[0], [(0, True, False)]), (BANK, pair[0], [(4, False, True)]),
                               (BANK, pair[1], [(0, True, False)])], RET_NORM - 1)
                half_chunk(base + 3, 1, pair[1])
                rot_transposes(0)
                for c in (2, 3):
                    pe.wait_ge(rot_ready, 2 * (c - 2) + 2)
                    half_chunk(base + 2 * c, 0, pair[c % 2])
                    rot_transposes(c - 1)
                    half_chunk(base + 2 * c + 1, 1, pair[c % 2])
                for h in range(RH):
                    if h == 0:
                        pe.wait_ge(rot_ready, 6)
                    else:
                        pe.wait_ge(rv_ready, 2 * h)
                    half_chunk(base + 8 + 4 * h, 0, pair[0])
                    if h == 0:
                        rot_transposes(3)
                    half_chunk(base + 9 + 4 * h, 1, pair[0])
                    if h:
                        gated_transposes(h - 1, [ps[4], ps[5]])
                    if h == 0:
                        pe.wait_ge(rot_ready, 8)
                    else:
                        pe.wait_ge(silu_g_ready, 2 * h)
                    half_chunk(base + 10 + 4 * h, 0, pair[1])
                    if h == 0:
                        pe.wait_ge(rqkT_ready, 4)
                        for head in range(RH):
                            ret_scores(head)
                    else:
                        ret_values(h)
                    half_chunk(base + 11 + 4 * h, 1, pair[1])
                    if h == 0:
                        ret_values(h)
                for d in range(6):
                    pe.wait_ge(gT_ready, RH - 1)
                    pe.wait_ge(yn_ready, 2 * RH)
                    output_slot(base + 24 + d, gT_hi, gT_lo, 2 * d, d == 0)
                    if d == 0:
                        gated_transposes(3, [ps[0], ps[1]])
                pe.wait_ge(gT_ready, RH)
                closing(base + 30, gT_hi, gT_lo, 12, RET_NORM)

            pe.wait_ge(ident_loaded, 16)
            pe.wait_ge(x_loaded[0], 16)
            x_transposes(0, 0, x_nat)
            ffn(0)
            attention()
            ffn(1)
            ffn(2)
            retention()
            ffn(3)

        @block.scalar
        def _(act):
            def split_hi(s, i=0):
                if s >= N_SLOTS:
                    return
                act.wait_ge(raw_loaded[s % RING], 16 * (s // RING + 1) + 16 * i)
                if s >= RING:
                    act.wait_ge(slots_used, used(s - RING) + RING * i)
                nc.scalar.activation(w_hi[:, s % RING, :], w_raw[:, s % RING, :], ACT.Copy).then_inc(hi_ready, 1)

            def first_slot_hi(k):
                act.wait_ge(first_raw[k] if k < 3 else raw_loaded[0], 16)
                at = slice(k * BANK, (k + 1) * BANK)
                nc.scalar.activation(w_hi[:, 0, at], w_raw[:, 0, at], ACT.Copy).then_inc(first_hi if k < 3 else hi_ready, 1)

            def first_x_hi(t):
                act.wait_ge(xT_psum, 2 * t + 2)
                nc.scalar.activation(xT_hi[:, 4:8, t * P:(t + 1) * P], ps[2 + t][:].rearrange("p (k q) -> p k q", k=4),
                                     ACT.Copy).then_inc(xT_b_hi, 1)

            def norm_hi(norm, t):
                number = NT * (norm + 1) + t
                act.wait_ge(xT_psum, 2 * number + 2)
                act.wait_ge(xT_ready, 2 * number)
                act.wait_ge(cols_loaded, 16)
                for k in range(4, 8):
                    done = nc.scalar.activation(xT_full[:, k, :], ps[2 + t][:, (k - 4) * P:(k - 3) * P], ACT.Identity,
                                                bias=cols[:, 1, norm, k:k + 1], scale=cols[:, 0, norm, k:k + 1])
                done.then_inc(xT_b_full, 1)
                act.wait_ge(xT_b_full, NT * norm + t + 1)
                nc.scalar.activation(xT_hi[:, 4:8, t * P:(t + 1) * P], xT_full[:, 4:8, :], ACT.Copy).then_inc(xT_b_hi, 1)

            def ffn(f):
                base = FFN_BASE[f]
                hT_hi, _, silu_gate, _ = ffn_bufs[f]

                def silu(c, i=0):
                    act.wait_ge(slots_used, used(base + 2 * c + 1) + RING * i)
                    if f or c:
                        act.wait_ge(h_ready, 2 * (NCH * f + c) + 4 * i)
                    for t in range(NT):
                        nc.scalar.activation(silu_gate[:, t, :], ps[2 * (c % 2) + t][:, 0:HC], ACT.Silu).then_inc(silu_ready, 1)

                def hidden_hi(c, bank, i=0):
                    act.wait_ge(hT_psum, NCH * f + c + 1 + 2 * i)
                    at = bass.ds(2 * c + 4 * i, 2) if not isinstance(i, int) else slice(2 * c, 2 * c + 2)
                    nc.scalar.activation(hT_hi[:, at, :], bank[:].rearrange("p (b q) -> p b q", b=2), ACT.Copy).then_inc(hT_hi_ready, 1)

                split_hi(base + 3)
                split_hi(base + 4)
                silu(0)
                split_hi(base + 5)
                split_hi(base + 6)
                hidden_hi(0, ps[4])
                with act.Fori(0, 4) as i:
                    for c in (2, 3):
                        silu(c - 1, i)
                        split_hi(base + 2 * c + 3, i)
                        hidden_hi(c - 1, ps[4 + (c - 1) % 2], i)
                        split_hi(base + 2 * c + 4, i)
                silu(NCH - 2)
                split_hi(base + 2 * NCH + 1)
                hidden_hi(NCH - 2, ps[5])
                split_hi(base + 2 * NCH + 2)
                silu(NCH - 1)
                split_hi(base + 2 * NCH + 3)
                hidden_hi(NCH - 1, ps[0])
                for s in range(2 * NCH + 4, FFN_SLOTS + 2):
                    split_hi(base + s)
                ending(FFN_NORM[f])

            def ending(norm):
                if norm == N_NORMS - 1:
                    return
                norm_hi(norm, 0)
                split_hi(END_SLOT[norm] + 2)
                norm_hi(norm, 1)

            def attention():
                base = ATT_BASE

                def q_copy(n):
                    act.wait_ge(slots_used, used(base + (2, 4)[n]))
                    if n:
                        act.wait_ge(qT_psum, 1)
                    for t in range(NT):
                        done = nc.scalar.activation(q_nat[:, t, :], ps[(2, 6)[n] + t][:], ACT.Copy)
                    done.then_inc(q_nat_ready, 1)

                def exps(b):
                    act.wait_ge(peaks_ready, b + 1)
                    for i, (c, w) in enumerate(((0, 256), (256, 256), (512, P), (640, P))):
                        nc.scalar.activation(probs[:, b % 4, c:c + w], probs[:, b % 4, c:c + w], ACT.Exp, scale=-1.0,
                                             bias=neg_peak[:, b % 4, i:i + 1], accum_out=sums[:, b % 4, i:i + 1])
                    nc.scalar.activation(sink_exp[:, b % 4, :], sink_less[:, b % 4, :], ACT.Exp).then_inc(exps_ready, 1)

                def pT1_copy(b):
                    act.wait_ge(pT_psum, b + 1)
                    if b == 4:
                        act.wait_ge(o_psum, 2)
                    nc.scalar.activation(pT1[:, :, :, b % 4, :].rearrange("p k j q -> p j k q"),
                                         ps[2][:].rearrange("p (j k q) -> p j k q", j=2, k=2), ACT.Copy).then_inc(pT1_ready, 1)

                def o_hi(g):
                    for t in range(NT):
                        act.wait_ge(o_psum, 2 * g + t + 1)
                        nc.scalar.activation(oT_hi[:, 4 * g:4 * g + 4, t * P:(t + 1) * P],
                                             O[g][t][:].rearrange("p (b q) -> p b q", b=4), ACT.Copy).then_inc(oT_hi_ready, 1)

                split_hi(base + 3)
                q_copy(0)
                act.wait_ge(kT_psum, 1)
                act.wait_ge(kz_ready, 1)
                act.wait_ge(att_consts, 16 * 5)
                for g in range(NKV):
                    for j in range(2):
                        rows = slice(j * DH, (j + 1) * DH)
                        done = nc.scalar.activation(kT[rows, g, j, :], ps[0][rows, g * SEQ:(g + 1) * SEQ], ACT.Identity,
                                                    bias=bq_col[rows, NB + g:NB + g + 1])
                done.then_inc(kT_ready, 1)
                split_hi(base + 4)
                split_hi(base + 5)
                split_hi(base + 6)
                for b in range(2):
                    exps(b)
                q_copy(1)
                for b in range(2, 4):
                    exps(b)
                for b in range(NB):
                    pT1_copy(b)
                    if b + 4 < NB:
                        exps(b + 4)
                    if b == 2:
                        split_hi(base + 7)
                    if b == 4:
                        o_hi(0)
                    if b == 3:
                        split_hi(base + 8)
                    if b == 6:
                        split_hi(base + 9)
                o_hi(1)
                split_hi(base + 10)
                ending(ATT_NORM)

            def retention():
                base = RET_BASE

                def rqk_copy(c):
                    act.wait_ge(rqkT_psum, c + 1)
                    for half in range(2):
                        done = nc.scalar.activation(rqkT[:, 4 * c + 2 * half:4 * c + 2 * half + 2, :],
                                                    ps[4 + half][:].rearrange("p (b q) -> p b q", b=2), ACT.Copy)
                    done.then_inc(rqkT_ready, 1)

                def v_copy(h):
                    act.wait_ge(slots_used, used(base + 9 + 4 * h))
                    if h:
                        act.wait_ge(ry_psum, h)
                    for t in range(NT):
                        nc.scalar.activation(rv[:, t, :], ps[t][:], ACT.Copy).then_inc(rv_ready, 1)

                def silu_of_g(h):
                    act.wait_ge(slots_used, used(base + 11 + 4 * h))
                    if h:
                        act.wait_ge(gated_ready, 2 * h)
                    for t in range(NT):
                        nc.scalar.activation(silu_g[:, t, :], ps[2 + t][:], ACT.Silu).then_inc(silu_g_ready, 1)

                def gated_hi(h, banks):
                    act.wait_ge(gT_psum, h + 1)
                    for half in range(2):
                        nc.scalar.activation(gT_hi[:, 4 * h + 2 * half:4 * h + 2 * half + 2, :],
                                             banks[half][:].rearrange("p (b q) -> p b q", b=2), ACT.Copy).then_inc(gT_hi_ready, 1)

                for s in (3, 4, 5, 6):
                    split_hi(base + s)
                rqk_copy(0)
                split_hi(base + 7)
                rqk_copy(1)
                split_hi(base + 8)
                split_hi(base + 9)
                rqk_copy(2)
                split_hi(base + 10)
                split_hi(base + 11)
                rqk_copy(3)
                for h in range(RH):
                    split_hi(base + 12 + 4 * h)
                    v_copy(h)
                    split_hi(base + 13 + 4 * h)
                    if h:
                        gated_hi(h - 1, [ps[4], ps[5]])
                    split_hi(base + 14 + 4 * h)
                    silu_of_g(h)
                    split_hi(base + 15 + 4 * h)
                gated_hi(RH - 1, [ps[0], ps[1]])
                for s in range(28, RET_SLOTS + 2):
                    split_hi(base + s)
                ending(RET_NORM)

            act.dma_start(x_nat[:, 0, :], x[0:P, :]).then_inc(x_loaded[0], 16)
            act.dma_start(ident[:], ident_in).then_inc(ident_loaded, 16)
            act.dma_start(x_nat[:, 1, :], x[P:2 * P, :]).then_inc(x_loaded[1], 16)
            first_slot_hi(0)
            first_x_hi(0)
            for k in range(1, 4):
                first_slot_hi(k)
            split_hi(1)
            split_hi(2)
            first_x_hi(1)
            ffn(0)
            attention()
            ffn(1)
            ffn(2)
            retention()
            ffn(3)

        @block.vector
        def _(dve):
            def split_lo(s, i=0):
                if s >= N_SLOTS:
                    return
                dve.wait_ge(hi_ready, s + 1 + RING * i)
                nc.vector.tensor_tensor(w_lo[:, s % RING, :], w_raw[:, s % RING, :], w_hi[:, s % RING, :],
                                        ALU.subtract).then_inc(lo_ready, 1)

            def first_slot_lo(k):
                dve.wait_ge(first_hi if k < 3 else hi_ready, min(k, 2) + 1 if k < 3 else 1)
                at = slice(k * BANK, (k + 1) * BANK)
                nc.vector.tensor_tensor(w_lo[:, 0, at], w_raw[:, 0, at], w_hi[:, 0, at],
                                        ALU.subtract).then_inc(first_lo if k < 3 else lo_ready, 1)

            def x_parts(number, t, source_a, source_b):
                tok = slice(t * P, (t + 1) * P)
                nc.vector.tensor_copy(xT_hi[:, 0:4, tok], source_a).then_inc(xT_a_hi, 1)
                dve.wait_ge(xT_a_hi, number + 1)
                nc.vector.tensor_tensor(xT_lo[:, 0:4, tok], source_a, xT_hi[:, 0:4, tok], ALU.subtract).then_inc(xT_ready, 1)
                dve.wait_ge(xT_b_hi, number + 1)
                nc.vector.tensor_tensor(xT_lo[:, 4:8, tok], source_b, xT_hi[:, 4:8, tok], ALU.subtract).then_inc(xT_ready, 1)

            def first_x(t):
                dve.wait_ge(xT_psum, 2 * t + 1)
                x_parts(t, t, *(ps[2 * half + t][:].rearrange("p (k q) -> p k q", k=4) for half in range(2)))

            def norm_sum(norm, t, n):
                index = NT * norm + t
                if (t, n) == (1, 1):
                    dve.wait_ge(slots_used, END_SLOT[norm])
                else:
                    dve.wait_ge(y_ready, 3 * norm + 2 * t + n + 1)
                if n == 0 and norm == 0:
                    dve.wait_ge(x_loaded[t], 16)
                elif n == 0:
                    dve.wait_ge(xnat_ready, index - 1)
                if n == 0 and norm == ATT_NORM:
                    dve.wait_ge(res_ready, t + 1)
                half = slice(n * BANK, (n + 1) * BANK)
                nc.vector.scalar_tensor_tensor(z[:, t, half], x_nat[:, t, half], 1.0 if norm == ATT_NORM else ALPHA,
                                               Y[t][n][:], ALU.mult, ALU.add).then_inc(sums_ready, 1)
                dve.wait_ge(sums_ready, 4 * index + 2 * n + 1)
                nc.vector.bn_stats(stats[:, t, n, :], z[:, t, half]).then_inc(sums_ready, 1)

            def norm_moments(norm, t):
                dve.wait_ge(sums_ready, 4 * (NT * norm + t) + 4)
                nc.vector.bn_aggr(moments[:, t, :], stats[:, t, :, :].rearrange("p a b -> p (a b)")).then_inc(stats_ready, 1)

            def norm_apply(norm, t):
                dve.wait_ge(rstd_ready, NT * norm + t + 1)
                for n in range(2):
                    half = slice(n * BANK, (n + 1) * BANK)
                    nc.vector.tensor_scalar(z[:, t, half], z[:, t, half], moments[:, t, 0:1], rstd[:, t, :],
                                            ALU.subtract, ALU.mult).then_inc(xhat_ready, 1)

            def norm_parts(norm, t):
                number = NT * (norm + 1) + t
                dve.wait_ge(xT_psum, 2 * number + 1)
                dve.wait_ge(cols_loaded, 16)
                dve.wait_ge(xT_ready, 2 * number)
                for k in range(4):
                    done = nc.vector.tensor_scalar(xT_full[:, k, :], ps[t][:, k * P:(k + 1) * P],
                                                   cols[:, 0, norm, k:k + 1], cols[:, 1, norm, k:k + 1], ALU.mult, ALU.add)
                done.then_inc(xT_a_full, 1)
                dve.wait_ge(xT_a_full, NT * norm + t + 1)
                x_parts(number, t, xT_full[:, 0:4, :], xT_full[:, 4:8, :])

            def ending(norm):
                if norm == N_NORMS - 1:
                    return
                for n in range(2):
                    norm_sum(norm, 0, n)
                norm_moments(norm, 0)
                norm_apply(norm, 0)
                norm_sum(norm, 1, 0)
                norm_parts(norm, 0)
                norm_sum(norm, 1, 1)
                norm_moments(norm, 1)
                split_lo(END_SLOT[norm] + 2)
                norm_apply(norm, 1)
                norm_parts(norm, 1)

            def last_norm():
                norm = N_NORMS - 1
                for t in range(NT):
                    for n in range(2):
                        norm_sum(norm, t, n)
                    norm_moments(norm, t)
                    dve.wait_ge(rows_loaded, 32 * N_NORMS)
                    dve.wait_ge(stats_ready, NT * norm + t + 1)
                    for n in range(2):
                        half = slice(n * BANK, (n + 1) * BANK)
                        nc.vector.scalar_tensor_tensor(z[:, t, half], z[:, t, half], moments[:, t, 0:1], gain_row[:, half],
                                                       ALU.subtract, ALU.mult).then_inc(out_step, 1)
                    dve.wait_ge(rstd_ready, NT * norm + t + 1)
                    for n in range(2):
                        half = slice(n * BANK, (n + 1) * BANK)
                        dve.wait_ge(out_step, 2 * t + n + 1)
                        nc.vector.scalar_tensor_tensor(z[:, t, half], z[:, t, half], rstd[:, t, :], bias_row[:, half],
                                                       ALU.mult, ALU.add).then_inc(out_ready, 1)

            def ffn(f):
                base = FFN_BASE[f]
                hT_hi, hT_lo, silu_gate, h_nat = ffn_bufs[f]

                def gate(c, i=0):
                    if f or c:
                        dve.wait_ge(hT_psum, NCH * f + c + 2 * i)
                    for t in range(NT):
                        dve.wait_ge(silu_ready, 2 * (NCH * f + c) + t + 1 + 4 * i)
                        nc.vector.scalar_tensor_tensor(h_nat[:, t, :], ps[2 * (c % 2) + t][:, HC:2 * HC], 0.5,
                                                       silu_gate[:, t, :], ALU.mult, ALU.mult).then_inc(h_ready, 1)

                def hidden_lo(c, bank, i=0):
                    dve.wait_ge(hT_hi_ready, NCH * f + c + 1 + 2 * i)
                    at = bass.ds(2 * c + 4 * i, 2) if not isinstance(i, int) else slice(2 * c, 2 * c + 2)
                    nc.vector.tensor_tensor(hT_lo[:, at, :], bank[:].rearrange("p (b q) -> p b q", b=2), hT_hi[:, at, :],
                                            ALU.subtract).then_inc(hT_ready, 1)

                split_lo(base + 3)
                split_lo(base + 4)
                gate(0)
                split_lo(base + 5)
                split_lo(base + 6)
                hidden_lo(0, ps[4])
                with dve.Fori(0, 4) as i:
                    for c in (2, 3):
                        gate(c - 1, i)
                        split_lo(base + 2 * c + 3, i)
                        hidden_lo(c - 1, ps[4 + (c - 1) % 2], i)
                        split_lo(base + 2 * c + 4, i)
                gate(NCH - 2)
                split_lo(base + 2 * NCH + 1)
                hidden_lo(NCH - 2, ps[5])
                split_lo(base + 2 * NCH + 2)
                gate(NCH - 1)
                split_lo(base + 2 * NCH + 3)
                hidden_lo(NCH - 1, ps[0])
                for s in range(2 * NCH + 4, FFN_SLOTS + 2):
                    split_lo(base + s)
                ending(FFN_NORM[f])

            def attention():
                base = ATT_BASE
                step = [0]

                def link(instruction):
                    step[0] += 1
                    instruction.then_inc(soft_step, 1)
                    dve.wait_ge(soft_step, step[0])

                def q_scaled(n):
                    dve.wait_ge(qT_psum, n + 1)
                    for b in range(4):
                        done = nc.vector.tensor_scalar(qT[:, 4 * n + b, :], ps[(2, 6)[n] + b // 2][:, (b % 2) * SEQ:(b % 2 + 1) * SEQ],
                                                       bq_col[:, 4 * n + b:4 * n + b + 1], -DH ** -0.5, ALU.add, ALU.mult)
                    done.then_inc(qT_ready, 1)

                def peaks(b):
                    bank1, bank0 = ((ps[4], ps[5]), (ps[0], ps[1]))[b % 2]
                    dve.wait_ge(scores_ready, b + 1)
                    if b >= 4:
                        dve.wait_ge(pT_psum, b - 3)
                    p1 = probs[:, b % 4, 0:512].rearrange("p (j k) -> p j k", j=2)
                    p0 = probs[:, b % 4, 512:768].rearrange("p (j k) -> p j k", j=2)
                    for j in range(2):
                        nc.vector.tensor_tensor_reduce(out=p1[:, j, :], in0=bank1[:, j * 256:(j + 1) * 256], in1=mask[:],
                                                       scale=1.0, scalar=neg_sink[:, b, j:j + 1], op0=ALU.add, op1=ALU.min,
                                                       accum_out=neg_peak[:, b % 4, j:j + 1])
                    for j in range(2):
                        done = nc.vector.tensor_tensor_reduce(out=p0[:, j, :], in0=bank0[:, j * P:(j + 1) * P],
                                                              in1=mask[:, P:2 * P], scale=1.0,
                                                              scalar=neg_sink[:, b, 2 + j:3 + j], op0=ALU.add, op1=ALU.min,
                                                              accum_out=neg_peak[:, b % 4, 2 + j:3 + j])
                    link(done)
                    nc.vector.tensor_tensor(sink_less[:, b % 4, :], neg_peak[:, b % 4, :], neg_sink[:, b, :],
                                            ALU.subtract).then_inc(peaks_ready, 1)

                def totals(b):
                    dve.wait_ge(exps_ready, b + 1)
                    link(nc.vector.tensor_tensor(total[:, b % 4, :], sums[:, b % 4, :], sink_exp[:, b % 4, :], ALU.add))
                    nc.vector.reciprocal(inv[:, b % 4, :], total[:, b % 4, :]).then_inc(inv_ready, 1)

                def pT0_copy(b):
                    dve.wait_ge(pT_psum, b + 1)
                    if b == 4:
                        dve.wait_ge(o_psum, 1)
                    nc.vector.tensor_copy(pT0[:, :, b % 4, :], ps[3][:, 0:256].rearrange("p (j q) -> p j q", j=2)).then_inc(pT0_ready, 1)

                def o_lo(g):
                    for t in range(NT):
                        dve.wait_ge(oT_hi_ready, 2 * g + t + 1)
                        at = (slice(None), slice(4 * g, 4 * g + 4), slice(t * P, (t + 1) * P))
                        nc.vector.tensor_tensor(oT_lo[at], O[g][t][:].rearrange("p (b q) -> p b q", b=4),
                                                oT_hi[at], ALU.subtract).then_inc(oT_ready, 1)

                nc.vector.memset(kT[:], 0.0).then_inc(kz_ready, 1)
                dve.wait_ge(att_consts, 16 * 5)
                link(nc.vector.tensor_scalar(neg_sink[:], sink[:], -1.0, None, ALU.mult))
                split_lo(base + 3)
                dve.wait_ge(slots_used, used(base))
                for t in range(NT):
                    for j in range(2):
                        nc.vector.tensor_copy(k_twice[:, t, :, j, :], ps[t][:, 0:P].rearrange("p (g d) -> p g d", g=NKV))
                    nc.vector.tensor_tensor(v_nat[:, t, :], ps[t][:, P:2 * P], bv_row[:], ALU.add).then_inc(kv_nat, 1)
                q_scaled(0)
                split_lo(base + 4)
                split_lo(base + 5)
                peaks(0)
                peaks(1)
                totals(0)
                split_lo(base + 6)
                totals(1)
                peaks(2)
                q_scaled(1)
                peaks(3)
                totals(2)
                for b in range(NB):
                    pT0_copy(b)
                    if b + 4 < NB:
                        peaks(b + 4)
                    if b + 3 < NB:
                        totals(b + 3)
                    if b == 3:
                        split_lo(base + 7)
                    if b == 4:
                        o_lo(0)
                    if b == 5:
                        split_lo(base + 8)
                    if b == 6:
                        split_lo(base + 9)
                o_lo(1)
                for t in range(NT):
                    dve.wait_ge(xnat_ready, t + 1)
                    nc.vector.scalar_tensor_tensor(x_nat[:, t, :], x_nat[:, t, :], ALPHA, bo_row[:], ALU.mult,
                                                   ALU.add).then_inc(res_ready, 1)
                split_lo(base + 10)
                ending(ATT_NORM)

            def retention():
                base = RET_BASE
                step = [0]

                def turn(c):
                    dve.wait_ge(slots_used, used(base + 2 * c + 1))
                    if c:
                        dve.wait_ge(rqkT_psum, c)
                    for t in range(NT):
                        halves = ps[2 * (c % 2) + t][:].rearrange("p (h f) -> p h f", f=P)
                        cos, sin = (rope[:, t, j:j + 1, :].broadcast_to([P, 4, P]) for j in range(2))
                        if c or t:
                            dve.wait_ge(rot_ready, 2 * c + t)
                        nc.vector.tensor_tensor(by_cos[:].rearrange("p (h f) -> p h f", f=P), halves, cos, ALU.mult)
                        nc.vector.tensor_tensor(by_sin[:].rearrange("p (h f) -> p h f", f=P), halves, sin,
                                                ALU.mult).then_inc(rot_step, 1)
                        c4, s4, r4 = (a.rearrange("p (h e f) -> p h e f", h=2, e=2) for a in (by_cos[:], by_sin[:], rot[:, t, :]))
                        dve.wait_ge(rot_step, step[0] + 1)
                        nc.vector.tensor_tensor(r4[:, :, 0, :], c4[:, :, 0, :], s4[:, :, 1, :], ALU.subtract).then_inc(rot_step, 1)
                        nc.vector.tensor_tensor(r4[:, :, 1, :], s4[:, :, 0, :], c4[:, :, 1, :], ALU.add).then_inc(rot_ready, 1)
                        step[0] += 2

                def decayed(h):
                    dve.wait_ge(scT_psum, h + 1)
                    nc.vector.tensor_tensor(scT[:, h, :], ps[6 + h % 2][:, 0:384], decay[:, h, :], ALU.mult).then_inc(scT_ready, 1)

                def group_stats(h):
                    dve.wait_ge(ry_psum, h + 1)
                    for t in range(NT):
                        nc.vector.bn_stats(gn_stats[:, t, :], ps[6 + t][:]).then_inc(gn_step, 1)
                    for t in range(NT):
                        dve.wait_ge(gn_step, 2 * h + t + 1)
                        nc.vector.bn_aggr(gn_moments[:, t, :], gn_stats[:, t, :]).then_inc(gn_stats_ready, 1)

                def group_norm(h):
                    dve.wait_ge(gn_rstd_ready, 2 * h + 2)
                    if h:
                        dve.wait_ge(gT_psum, h)
                    for t in range(NT):
                        nc.vector.tensor_scalar(y_nat[:, t, :], ps[6 + t][:], gn_moments[:, t, 0:1], gn_rstd[:, t, :],
                                                ALU.subtract, ALU.mult).then_inc(yn_ready, 1)

                def gated(h):
                    for t in range(NT):
                        dve.wait_ge(silu_g_ready, 2 * h + t + 1)
                        dve.wait_ge(yn_ready, 2 * h + t + 1)
                        nc.vector.tensor_tensor(y_nat[:, t, :], y_nat[:, t, :], silu_g[:, t, :], ALU.mult).then_inc(gated_ready, 1)

                def gated_lo(h, banks):
                    for half in range(2):
                        dve.wait_ge(gT_hi_ready, 2 * h + half + 1)
                        at = slice(4 * h + 2 * half, 4 * h + 2 * half + 2)
                        done = nc.vector.tensor_tensor(gT_lo[:, at, :], banks[half][:].rearrange("p (b q) -> p b q", b=2),
                                                       gT_hi[:, at, :], ALU.subtract)
                    done.then_inc(gT_ready, 1)

                split_lo(base + 3)
                split_lo(base + 4)
                dve.wait_ge(ret_consts, 32)
                turn(0)
                split_lo(base + 5)
                split_lo(base + 6)
                turn(1)
                split_lo(base + 7)
                split_lo(base + 8)
                turn(2)
                split_lo(base + 9)
                split_lo(base + 10)
                turn(3)
                split_lo(base + 11)
                for h in range(RH):
                    split_lo(base + 12 + 4 * h)
                    if h == 0:
                        for head in range(RH):
                            decayed(head)
                    split_lo(base + 13 + 4 * h)
                    if h:
                        gated_lo(h - 1, [ps[4], ps[5]])
                    group_stats(h)
                    group_norm(h)
                    split_lo(base + 14 + 4 * h)
                    gated(h)
                    split_lo(base + 15 + 4 * h)
                gated_lo(RH - 1, [ps[0], ps[1]])
                for s in range(28, RET_SLOTS + 2):
                    split_lo(base + s)
                ending(RET_NORM)

            first_x(0)
            for k in range(4):
                first_slot_lo(k)
            split_lo(1)
            split_lo(2)
            first_x(1)
            ffn(0)
            attention()
            ffn(1)
            ffn(2)
            retention()
            ffn(3)
            last_norm()

        @block.gpsimd
        def _(pool):
            def rows_for(norm):
                for j, row in enumerate((gain_row, bias_row)):
                    pool.dma_start(row[:], norm_rows[j, norm:norm + 1, :].broadcast_to([P, D])).then_inc(rows_loaded, 16)

            def reciprocal_roots(norm):
                for t in range(NT):
                    index = NT * norm + t
                    pool.wait_ge(stats_ready, index + 1)
                    nc.gpsimd.tensor_tensor(rstd[:, t, :], moments[:, t, 1:2], eps_pow[:, 0:1], ALU.add).then_inc(var_ready, 1)
                    pool.wait_ge(var_ready, index + 1)
                    nc.gpsimd.tensor_tensor(rstd[:, t, :], rstd[:, t, :], eps_pow[:, 2:3], ALU.pow).then_inc(rstd_ready, 1)

            def residual(norm):
                pool.wait_ge(rows_loaded, 32 * (norm + 1))
                for t in range(NT):
                    index = NT * norm + t
                    pool.wait_ge(xhat_ready, 2 * index + 2)
                    nc.gpsimd.tensor_tensor(x_nat[:, t, :], z[:, t, :], gain_row[:], ALU.mult).then_inc(x_scaled, 1)
                    pool.wait_ge(x_scaled, index + 1)
                    nc.gpsimd.tensor_tensor(x_nat[:, t, :], x_nat[:, t, :], bias_row[:], ALU.add).then_inc(xnat_ready, 1)

            def norm_of(norm, loads=None):
                reciprocal_roots(norm)
                if loads:
                    pool.wait_ge(slots_used, END_SLOT[norm])
                    loads()
                if norm < N_NORMS - 1:
                    residual(norm)
                    pool.wait_ge(xnat_ready, NT * (norm + 1))
                    rows_for(norm + 1)

            def attention_constants():
                pool.dma_start(mask[:], mask_in).then_inc(att_consts, 16)
                pool.dma_start(bq_col[:], att_cols).then_inc(att_consts, 16)
                pool.dma_start(sink[:], sinks).then_inc(att_consts, 16)
                pool.dma_start(bv_row[:], att_rows[0:1, D:D + NKV * DH].broadcast_to([P, NKV * DH])).then_inc(att_consts, 16)
                pool.dma_start(bo_row[:], att_rows[0:1, 0:D].broadcast_to([P, D])).then_inc(att_consts, 16)

            def retention_constants():
                pool.dma_start(rope[:], rope_in).then_inc(ret_consts, 16)
                pool.dma_start(decay[:], decay_in).then_inc(ret_consts, 16)

            nc.gpsimd.memset(eps_pow[:, 0:1], LN_EPS)
            nc.gpsimd.memset(eps_pow[:, 1:2], GN_EPS)
            nc.gpsimd.memset(eps_pow[:, 2:3], -0.5).then_inc(eps_ready, 1)
            pool.wait_ge(eps_ready, 1)
            rows_for(0)
            norm_of(0, attention_constants)
            for b in range(NB):
                pool.wait_ge(inv_ready, b + 1)
                for at, i, w in ((0, 0, 2 * P), (4 * P, 2, P)):
                    p = probs[:, b % 4, at:at + 2 * w].rearrange("p (j k) -> p j k", j=2)
                    done = nc.gpsimd.tensor_tensor(p, p, inv[:, b % 4, i:i + 2, None].broadcast_to([P, 2, w]), ALU.mult)
                done.then_inc(probs_ready, 1)
            norm_of(1)
            norm_of(2)
            norm_of(3, retention_constants)
            for h in range(RH):
                for t in range(NT):
                    index = NT * h + t
                    pool.wait_ge(gn_stats_ready, index + 1)
                    nc.gpsimd.tensor_tensor(gn_rstd[:, t, :], gn_moments[:, t, 1:2], eps_pow[:, 1:2], ALU.add).then_inc(gn_var, 1)
                    pool.wait_ge(gn_var, index + 1)
                    nc.gpsimd.tensor_tensor(gn_rstd[:, t, :], gn_rstd[:, t, :], eps_pow[:, 2:3], ALU.pow).then_inc(gn_rstd_ready, 1)
            norm_of(4)
            norm_of(5)


def pack_slots(w, columns):
    import numpy as np
    k = w.shape[0] // P
    blocks = w.reshape(k, P, -1)[:, :, columns]
    per_slot = SLOT // len(columns)
    assert k % per_slot == 0
    return np.transpose(blocks.reshape(k // per_slot, per_slot, P, len(columns)), (0, 2, 1, 3)).reshape(-1, P, SLOT)


def kernel(x, ln_g, ln_b, ffn1_w_gate_up, ffn1_w_down, ffn2_w_gate_up, ffn2_w_down,
           attn_w_qkv, attn_b_qkv, attn_sinks, attn_w_o, attn_b_o, ret_w_qkvg, ret_w_o):
    import numpy as np
    import concourse.bacc as bacc
    from concourse.bass_utils import run_bass_kernel_spmd

    slots = []

    def add_ffn(w_gate_up, w_down):
        for c in range(NCH):
            at = np.arange(c * HC, (c + 1) * HC)
            slots.append(pack_slots(w_gate_up, np.concatenate([at, FFN + at])))
        slots.append(pack_slots(w_down, np.arange(D)))

    add_ffn(ffn1_w_gate_up[0], ffn1_w_down[0])
    slots.append(pack_slots(attn_w_qkv[0], np.arange(D, D + 256)))
    for n in range(2):
        slots.append(pack_slots(attn_w_qkv[0], np.arange(n * BANK, (n + 1) * BANK)))
    slots.append(pack_slots(attn_w_o[0], np.arange(D)))
    add_ffn(ffn2_w_gate_up[0], ffn2_w_down[0])
    add_ffn(ffn1_w_gate_up[1], ffn1_w_down[1])
    order = [0, 1, 2, 3] + [c for h in range(RH) for c in (4 + h, 8 + h)]
    for c in order:
        slots.append(pack_slots(ret_w_qkvg[0], np.arange(c * BANK, (c + 1) * BANK)))
    slots.append(pack_slots(ret_w_o[0], np.arange(D)))
    add_ffn(ffn2_w_gate_up[1], ffn2_w_down[1])
    weights = np.concatenate(slots).reshape(-1, SLOT)
    assert weights.shape[0] == N_SLOTS * P

    norm_rows = np.stack([ln_g.reshape(N_NORMS, D), ln_b.reshape(N_NORMS, D)])
    norm_cols = np.transpose(norm_rows.reshape(2, N_NORMS, KD, P), (3, 0, 1, 2))
    b = attn_b_qkv[0]
    bias_q = b[:D].reshape(NB, P)
    bias_k = b[D:D + NKV * DH].reshape(NKV, 1, DH)
    att_cols = np.concatenate([bias_q, np.repeat(bias_k, 2, axis=1).reshape(NKV, P)]).T
    pairs = attn_sinks[0].reshape(NB, 2)
    sinks = np.broadcast_to(np.concatenate([pairs, pairs], axis=1)[None], (P, NB, 4))
    att_rows = np.concatenate([attn_b_o[0], b[D + NKV * DH:]])[None]

    f = np.float32
    row, col = np.arange(P)[:, None], np.arange(P)[None, :]
    ident = np.eye(P, dtype=f)
    mask = np.concatenate([np.where(col > row, 0.0, 1e30), np.where(col <= row, 0.0, 1e30)], axis=1).astype(f)
    freqs = (f(1.0) / (f(10000.0) ** np.linspace(0.0, 1.0, P, dtype=f))).astype(f)
    angle = (np.arange(SEQ, dtype=f)[:, None] * freqs[None, :]).astype(np.float64)
    rope = np.stack([np.cos(angle), np.sin(angle)], axis=1).astype(f).reshape(NT, P, 2, P).transpose(1, 0, 2, 3)
    gamma = 1.0 - 2.0 ** (-5.0 - np.arange(RH))
    ahead = np.concatenate([col - row, col + P - row, col - row], axis=1)
    decay = np.where(ahead >= 0, gamma[:, None, None] ** np.maximum(ahead, 0), 0.0) * RQ ** -0.5
    decay = decay.transpose(1, 0, 2).astype(f)

    arrays = {"x": x.reshape(SEQ, D), "weights": weights, "norm_rows": norm_rows, "norm_cols": norm_cols,
              "att_cols": att_cols, "sinks": sinks, "att_rows": att_rows, "ident_in": ident, "mask_in": mask,
              "rope_in": rope, "decay_in": decay}
    arrays = {n: np.ascontiguousarray(a) for n, a in arrays.items()}
    nc = bacc.Bacc("TRN2", target_bir_lowering=False, num_devices=1)
    f32 = mybir.dt.float32
    handles = {n: nc.dram_tensor(n, a.shape, f32, kind="ExternalInput").ap() for n, a in arrays.items()}
    out = nc.dram_tensor("out", (SEQ, D), f32, kind="ExternalOutput").ap()
    trunk(nc, out=out, **handles)
    result = run_bass_kernel_spmd(nc, [arrays], core_ids=[0])
    return result.results[0]["out"].reshape(1, SEQ, D)
```

```python
import concourse.bass as bass
from concourse import mybir
from contextlib import ExitStack

P = 128
D = 1024
SEQ = 256
NT = SEQ // P
KD = D // P
FFN = 2816
HC = 256
NCH = FFN // HC
KF = FFN // P
NH, NKV, DH = 16, 2, 64
NB = NH // 2
RH, RQ, RV = 4, 256, 512
SLOT = 2048
RING = 4
BANK = 512
ALPHA = (2.0 * 2) ** 0.25
LN_EPS, GN_EPS = 1e-5, 1e-6

FFN_SLOTS = 2 * NCH + KF // 2
ATT_SLOTS = 1 + 4 + 4
RET_SLOTS = 24 + 8
FFN_BASE = [0, FFN_SLOTS + ATT_SLOTS, 2 * FFN_SLOTS + ATT_SLOTS, 3 * FFN_SLOTS + ATT_SLOTS + RET_SLOTS]
ATT_BASE = FFN_SLOTS
RET_BASE = 3 * FFN_SLOTS + ATT_SLOTS
N_SLOTS = 4 * FFN_SLOTS + ATT_SLOTS + RET_SLOTS
FFN_NORM = [0, 2, 3, 5]
ATT_NORM, RET_NORM = 1, 4
N_NORMS = 6
END_SLOT = [FFN_SLOTS, ATT_BASE + ATT_SLOTS, FFN_BASE[1] + FFN_SLOTS, FFN_BASE[2] + FFN_SLOTS,
            RET_BASE + RET_SLOTS, N_SLOTS]

NORMED_BY_SCALAR = [(norm, t) for norm in range(N_NORMS - 1) for t in range(NT) if t or norm == ATT_NORM]
HALVED = [1, 2] + [s + 2 for s in END_SLOT[:-1]]


def trunk(nc, x, weights, norm_rows, norm_cols, att_cols, sinks, att_rows, ident_in, mask_in, rope_in, decay_in, out):
    f32 = mybir.dt.float32
    f32r = mybir.dt.float32r
    ALU = mybir.AluOpType
    ACT = mybir.ActivationFunctionType

    ctx = ExitStack()
    with ctx:
        def sb(name, shape, dt=f32, within=ctx):
            return within.enter_context(nc.sbuf_tensor(name, shape, dt))

        def sem(name):
            return ctx.enter_context(nc.semaphore(name))

        w_raw = sb("w_raw", [P, RING, SLOT])
        w_hi = sb("w_hi", [P, RING, SLOT], f32r)
        w_lo = sb("w_lo", [P, RING, SLOT], f32r)
        xT_hi = sb("xT_hi", [P, KD, SEQ], f32r)
        xT_lo = sb("xT_lo", [P, KD, SEQ], f32r)
        x_nat = sb("x_nat", [P, NT, D])
        z = sb("z", [P, NT, D])
        xT_full = sb("xT_full", [P, KD, P])
        gain_row = sb("gain_row", [P, D])
        bias_row = sb("bias_row", [P, D])
        cols = sb("cols", [P, 2, N_NORMS, KD])
        stats = sb("stats", [P, NT, 2, 6])
        moments = sb("moments", [P, NT, 2])
        rstd = sb("rstd", [P, NT, 1])
        shift = sb("shift", [P, NT])
        eps_pow = sb("eps_pow", [P, 3])
        ident = sb("ident", [P, P])
        gn_stats = sb("gn_stats", [P, NT, 6])
        gn_moments = sb("gn_moments", [P, NT, 2])
        gn_rstd = sb("gn_rstd", [P, NT, 1])

        def ffn_tensors(f):
            with ExitStack() as r:
                return [sb(f"{n}{f}", s, d, r) for n, s, d in (
                    ("hT_hi", [P, KF, SEQ], f32r), ("hT_lo", [P, KF, SEQ], f32r),
                    ("silu_gate", [P, NT, HC], f32), ("h_nat", [P, NT, HC], f32))]

        ffn_bufs = [ffn_tensors(f) for f in range(4)]
        with ExitStack() as r:
            oT_hi = sb("oT_hi", [P, NB, SEQ], f32r, r)
            oT_lo = sb("oT_lo", [P, NB, SEQ], f32r, r)
            q_nat = sb("q_nat", [P, NT, BANK], f32, r)
            qT = sb("qT", [P, NB, SEQ], f32, r)
            k_twice = sb("k_twice", [P, NT, NKV, 2, DH], f32, r)
            kT = sb("kT", [P, NKV, 2, SEQ], f32, r)
            v_nat = sb("v_nat", [P, NT, NKV * DH], f32, r)
            probs = sb("probs", [P, 4, 768], f32, r)
            pT1 = sb("pT1", [P, 2, 2, 4, P], f32, r)
            pT0 = sb("pT0", [P, 2, 4, P], f32, r)
            mask = sb("mask", [P, 2 * P], f32, r)
            bo_row = sb("bo_row", [P, D], f32, r)
            bv_row = sb("bv_row", [P, NKV * DH], f32, r)
            bq_col = sb("bq_col", [P, NB + NKV], f32, r)
            sink = sb("sink", [P, NB, 4], f32, r)
            neg_sink = sb("neg_sink", [P, NB, 4], f32, r)
            neg_peak = sb("neg_peak", [P, 4, 4], f32, r)
            sink_less = sb("sink_less", [P, 4, 4], f32, r)
            sink_exp = sb("sink_exp", [P, 4, 4], f32, r)
            sums = sb("sums", [P, 4, 4], f32, r)
            total = sb("total", [P, 4, 4], f32, r)
            inv = sb("inv", [P, 4, 4], f32, r)
        with ExitStack() as r:
            scT_hi = sb("scT_hi", [P, RH, 384], f32r, r)
            scT_lo = sb("scT_lo", [P, RH, 384], f32r, r)
            rv_hi = sb("rv_hi", [P, NT, RV], f32r, r)
            rv_lo = sb("rv_lo", [P, NT, RV], f32r, r)
            silu_g = sb("silu_g", [P, NT, RV], f32, r)
            y_nat = sb("y_nat", [P, NT, RV], f32, r)
            decay = sb("decay", [P, RH, 384], f32, r)
            with ExitStack() as early:
                rqkT = sb("rqkT", [P, 16, SEQ], f32, early)
                by_cos = sb("by_cos", [P, BANK], f32, early)
                by_sin = sb("by_sin", [P, BANK], f32, early)
                rot = sb("rot", [P, NT, BANK], f32, early)
                rope = sb("rope", [P, NT, 2, P], f32, early)
                scT = sb("scT", [P, RH, 384], f32, early)
            gT_hi = sb("gT_hi", [P, 16, SEQ], f32r, r)
            gT_lo = sb("gT_lo", [P, 16, SEQ], f32r, r)

        ps = [ctx.enter_context(nc.psum_tensor(f"bank{b}", [P, BANK], f32)) for b in range(8)]
        O = [[ps[7], ps[6]], [ps[1], ps[0]]]
        Y = [[ps[4 + 2 * t + n] for n in range(2)] for t in range(NT)]

        first_raw = [sem(f"first_raw{i}") for i in range(3)]
        first_hi = sem("first_hi")
        first_lo = sem("first_lo")
        raw_loaded = [sem(f"raw_loaded{i}") for i in range(RING)]
        x_loaded = [sem(f"x_loaded{t}") for t in range(NT)]
        ident_loaded = sem("ident_loaded")
        cols_loaded = sem("cols_loaded")
        rows_loaded = sem("rows_loaded")
        att_consts = sem("att_consts")
        ret_consts = sem("ret_consts")
        half_hi = sem("half_hi")
        half_lo = sem("half_lo")
        hi_ready = sem("hi_ready")
        lo_ready = sem("lo_ready")
        slots_used = sem("slots_used")
        y_ready = sem("y_ready")
        sums_ready = sem("sums_ready")
        stats_ready = sem("stats_ready")
        var_ready = sem("var_ready")
        rstd_ready = sem("rstd_ready")
        shift_ready = sem("shift_ready")
        xhat_ready = sem("xhat_ready")
        xT_psum = sem("xT_psum")
        xT_a_full = sem("xT_a_full")
        xT_a_hi = sem("xT_a_hi")
        xT_b_full = sem("xT_b_full")
        xT_b_hi = sem("xT_b_hi")
        xT_a_ready = sem("xT_a_ready")
        xT_b_ready = sem("xT_b_ready")
        x_scaled = sem("x_scaled")
        xnat_ready = sem("xnat_ready")
        res_scaled = sem("res_scaled")
        res_ready = sem("res_ready")
        eps_ready = sem("eps_ready")
        silu_ready = sem("silu_ready")
        h_ready = sem("h_ready")
        hT_psum = sem("hT_psum")
        hT_hi_ready = sem("hT_hi_ready")
        hT_ready = sem("hT_ready")
        kz_ready = sem("kz_ready")
        kv_nat = sem("kv_nat")
        kT_psum = sem("kT_psum")
        kT_ready = sem("kT_ready")
        q_nat_ready = sem("q_nat_ready")
        qT_psum = sem("qT_psum")
        qT_ready = sem("qT_ready")
        scores_ready = sem("scores_ready")
        soft_step = sem("soft_step")
        peaks_ready = sem("peaks_ready")
        exps_ready = sem("exps_ready")
        inv_ready = sem("inv_ready")
        probs_ready = sem("probs_ready")
        pT_psum = sem("pT_psum")
        pT1_ready = sem("pT1_ready")
        pT0_ready = sem("pT0_ready")
        o_psum = sem("o_psum")
        oT_hi_ready = sem("oT_hi_ready")
        oT_ready = sem("oT_ready")
        rot_step = sem("rot_step")
        rot_ready = sem("rot_ready")
        rqkT_psum = sem("rqkT_psum")
        rqkT_ready = sem("rqkT_ready")
        scT_psum = sem("scT_psum")
        scT_ready = sem("scT_ready")
        scT_step = sem("scT_step")
        rv_hi_ready = sem("rv_hi_ready")
        rv_ready = sem("rv_ready")
        ry_psum = sem("ry_psum")
        gn_step = sem("gn_step")
        gn_stats_ready = sem("gn_stats_ready")
        gn_var = sem("gn_var")
        gn_rstd_ready = sem("gn_rstd_ready")
        yn_ready = sem("yn_ready")
        silu_g_ready = sem("silu_g_ready")
        gated_ready = sem("gated_ready")
        gT_psum = sem("gT_psum")
        gT_hi_ready = sem("gT_hi_ready")
        gT_ready = sem("gT_ready")
        out_step = sem("out_step")
        out_ready = sem("out_ready")
        out_stored = sem("out_stored")

        def used(s):
            return s + 1

        block = ctx.enter_context(nc.Block())

        @block.sync
        def _(sp):
            def load(s, i=0):
                if s >= RING:
                    sp.wait_ge(lo_ready, s - RING + 1 + RING * i)
                sp.dma_start(w_raw[:, s % RING, :], weights[bass.ds((s + RING * i) * P, P), :]).then_inc(raw_loaded[s % RING], 16)

            sp.dma_start(x_nat[:, 0, :], x[0:P, :]).then_inc(x_loaded[0], 16)
            for k in range(4):
                at = slice(k * BANK, (k + 1) * BANK)
                sp.dma_start(w_raw[:, 0, at], weights[0:P, at]).then_inc(first_raw[k] if k < 3 else raw_loaded[0], 16)
            load(1)
            load(2)
            sp.dma_start(x_nat[:, 1, :], x[P:2 * P, :]).then_inc(x_loaded[1], 16)
            load(3)
            sp.dma_start(cols[:], norm_cols).then_inc(cols_loaded, 16)
            with sp.Fori(0, N_SLOTS // RING - 1) as i:
                for s in range(RING, 2 * RING):
                    load(s, i)
            for s in range(N_SLOTS // RING * RING, N_SLOTS):
                load(s)
            for t in range(NT):
                for n in range(2):
                    sp.wait_ge(out_ready, 2 * t + n + 1)
                    sp.dma_start(out[t * P:(t + 1) * P, n * BANK:(n + 1) * BANK],
                                 z[:, t, n * BANK:(n + 1) * BANK]).then_inc(out_stored, 16)
            sp.wait_ge(out_stored, 16 * 2 * NT)

        @block.tensor
        def _(pe):
            def three(bank, hi, lo, whi, wlo, start, stop):
                nc.tensor.matmul(bank, hi, whi, start=start, stop=False)
                nc.tensor.matmul(bank, hi, wlo, start=False, stop=False)
                return nc.tensor.matmul(bank, lo, whi, start=False, stop=stop)

            def part(s, t, width, act_hi, act_lo, k, at, banks, start, stop, halves=None):
                tok = slice(t * P, (t + 1) * P)
                for n in halves or range(len(banks)):
                    w = slice(at * width + n * BANK, at * width + min(width, (n + 1) * BANK))
                    done = three(banks[n][:, 0:min(width, BANK)], act_hi[:, k, tok], act_lo[:, k, tok],
                                 w_hi[:, s % RING, w], w_lo[:, s % RING, w], start, stop)
                return done

            def wait_slot(s, i=0):
                pe.wait_ge(lo_ready, s + 1 + RING * i)

            def x_transposes(number, t, src):
                if number >= NT:
                    pe.wait_ge(xhat_ready, 2 * (number - NT) + 2)
                for half in range(2):
                    for i, k in enumerate((0, 1, 4, 5)):
                        f = slice((2 * half + k) * P, (2 * half + k + 1) * P)
                        done = nc.tensor.transpose(Y[t][half][:, i * P:(i + 1) * P], src[:, t, f], ident[:])
                    done.then_inc(xT_psum, 1)

            def norm_number(norm, t):
                return NT * (norm + 1) + t

            def opening(base, spec, norm):
                for t in range(NT):
                    number = norm_number(norm, t)
                    for j, (width, banks, parts) in enumerate(spec):
                        halved = base + j in HALVED
                        if t == 0 and halved:
                            pe.wait_ge(half_lo, HALVED.index(base + j) + 1)
                        elif t == 0 and base + j > 0:
                            wait_slot(base + j)
                        for k0, first, last in parts:
                            for k in range(4):
                                if t == 0 and halved and k == 2:
                                    wait_slot(base + j)
                                if (t, j, k) == (0, 2, 1):
                                    if norm < 0:
                                        pe.wait_ge(x_loaded[1], 16)
                                    x_transposes(norm_number(norm, 1), 1, x_nat if norm < 0 else z)
                                if k % 2 == 0 and (j, k0) in ((0, 0), (0, 4), (1, 4)):
                                    pe.wait_ge(xT_b_ready if k else xT_a_ready, 2 * number + 1 + k0 // 4)
                                if t == 0 and base + j == 0:
                                    pe.wait_ge(*((first_lo, k + 1) if k < 3 else (lo_ready, 1)))
                                done = part(base + j, t, width, xT_hi, xT_lo, k0 + k, k0 + k - parts[0][0], [banks[t]],
                                            first and k == 0, last and k == 3)
                        if t == 1:
                            done.then_inc(slots_used, 1)

            def closing(base, act_hi, act_lo, k0, norm, parted=None):
                for t in range(NT):
                    if parted:
                        pe.wait_ge(oT_ready, parted + t + 1)
                    for n in range(2):
                        for j in range(2):
                            if t == 0 and n == 0:
                                wait_slot(base + j)
                            if t == 1 and n == 1 and j == 1 and norm < N_NORMS - 1:
                                x_transposes(norm_number(norm, 0), 0, z)
                            for k in range(2):
                                done = part(base + j, t, D, act_hi, act_lo, k0 + 2 * j + k, k, Y[t], False,
                                            j == 1 and k == 1, halves=(n,))
                            if t == 1 and n == 1:
                                done.then_inc(slots_used, 1)
                        if (t, n) != (1, 1):
                            done.then_inc(y_ready, 1)

            def output_slot(s, act_hi, act_lo, k0, first, early=None, between=None):
                wait_slot(s)
                for t in range(NT):
                    if t and between:
                        between()
                    for k in range(2):
                        if (t, k) == (0, 1) and early:
                            early()
                        done = part(s, t, D, act_hi, act_lo, k0 + k, k, Y[t], first and k == 0, False)
                done.then_inc(slots_used, 1)

            def half_chunk(s, half, banks, i=0, between=None):
                wait_slot(s, i)
                for t in range(NT):
                    if t and between:
                        between()
                    for k in range(4):
                        done = part(s, t, BANK, xT_hi, xT_lo, 4 * half + k, k, [banks[t]],
                                    half == 0 and k == 0, half == 1 and k == 3)
                done.then_inc(slots_used, 1)

            def ffn(f):
                base = FFN_BASE[f]
                hT_hi, hT_lo, _, h_nat = ffn_bufs[f]
                pair = [[ps[0], ps[1]], [ps[2], ps[3]]]

                def h_transposes(c, bank, i=0):
                    pe.wait_ge(h_ready, 2 * (NCH * f + c) + 2 + 4 * i)
                    for b in range(2):
                        for t in range(NT):
                            done = nc.tensor.transpose(bank[:, (2 * b + t) * P:(2 * b + t + 1) * P],
                                                       h_nat[:, t, b * P:(b + 1) * P], ident[:])
                    done.then_inc(hT_psum, 1)

                opening(base, [(BANK, pair[0], [(0, True, False)]), (BANK, pair[0], [(4, False, True)]),
                               (BANK, pair[1], [(0, True, False)])], FFN_NORM[f] - 1)
                half_chunk(base + 3, 1, pair[1])
                h_transposes(0, ps[4])
                with pe.Fori(0, 4) as i:
                    for c in (2, 3):
                        pe.wait_ge(h_ready, 2 * (NCH * f + c - 2) + 2 + 4 * i)
                        half_chunk(base + 2 * c, 0, pair[c % 2], i)
                        h_transposes(c - 1, ps[4 + (c - 1) % 2], i)
                        half_chunk(base + 2 * c + 1, 1, pair[c % 2], i)
                pe.wait_ge(h_ready, 2 * (NCH * f + NCH - 3) + 2)
                half_chunk(base + 2 * NCH - 2, 0, pair[0])
                h_transposes(NCH - 2, ps[5])
                half_chunk(base + 2 * NCH - 1, 1, pair[0])
                down = base + 2 * NCH
                for d in range(NCH - 2):
                    pe.wait_ge(hT_ready, NCH * f + NCH - 1)
                    output_slot(down + d, hT_hi, hT_lo, 2 * d, d == 0)
                    if d == 0:
                        h_transposes(NCH - 1, ps[0])
                pe.wait_ge(hT_ready, NCH * f + NCH)
                closing(down + NCH - 2, hT_hi, hT_lo, 2 * (NCH - 2), FFN_NORM[f])

            def attention():
                base = ATT_BASE
                opening(base, [(256, [ps[0], ps[1]], [(0, True, False), (4, False, True)]),
                               (BANK, [ps[2], ps[3]], [(0, True, False)]),
                               (BANK, [ps[2], ps[3]], [(4, False, True)])], ATT_NORM - 1)

                def k_transposes():
                    pe.wait_ge(kv_nat, NT)
                    for g in range(NKV):
                        for t in range(NT):
                            done = nc.tensor.transpose(ps[0][:, (2 * g + t) * P:(2 * g + t + 1) * P],
                                                       k_twice[:, t, g, :, :].rearrange("p a b -> p (a b)"), ident[:])
                    done.then_inc(kT_psum, 1)

                def q_transposes(n):
                    pe.wait_ge(q_nat_ready, n + 1)
                    for b in range(4):
                        for t in range(NT):
                            c = (2 * (b % 2) + t) * P
                            done = nc.tensor.transpose(ps[(2, 6)[n] + b // 2][:, c:c + P], q_nat[:, t, b * P:(b + 1) * P], ident[:])
                    done.then_inc(qT_psum, 1)

                def scores(b):
                    bank1, bank0 = ((ps[4], ps[5]), (ps[0], ps[1]))[b % 2]
                    if b == 0:
                        pe.wait_ge(kT_ready, 1)
                    if b % 4 == 0:
                        pe.wait_ge(qT_ready, b // 4 + 1)
                    if b >= 2:
                        pe.wait_ge(peaks_ready, b - 1)
                    g = b // 4
                    nc.tensor.matmul(bank1[:], qT[:, b, P:2 * P], kT[:, g, :, :].rearrange("p j k -> p (j k)"),
                                     start=True, stop=True)
                    nc.tensor.matmul(bank0[:, 0:2 * P], qT[:, b, 0:P], kT[:, g, :, 0:P],
                                     start=True, stop=True).then_inc(scores_ready, 1)

                def p_transposes(b):
                    pe.wait_ge(probs_ready, b + 1)
                    if b == 0:
                        pe.wait_ge(qT_ready, 1)
                    else:
                        pe.wait_ge(pT1_ready, b)
                        pe.wait_ge(pT0_ready, b)
                    for j in range(2):
                        for kb in range(2):
                            nc.tensor.transpose(ps[2][:, (2 * j + kb) * P:(2 * j + kb + 1) * P],
                                                probs[:, b % 4, j * 256 + kb * P:j * 256 + (kb + 1) * P], ident[:])
                    for j in range(2):
                        done = nc.tensor.transpose(ps[3][:, j * P:(j + 1) * P],
                                                   probs[:, b % 4, 512 + j * P:512 + (j + 1) * P], ident[:])
                    done.then_inc(pT_psum, 1)

                def values(g):
                    pe.wait_ge(pT1_ready, 4 * g + 4)
                    pe.wait_ge(pT0_ready, 4 * g + 4)
                    if g:
                        pe.wait_ge(peaks_ready, NB)
                    v = [v_nat[:, t, g * DH:(g + 1) * DH] for t in range(NT)]
                    o0, o1 = O[g]
                    for j in range(2):
                        done = nc.tensor.matmul(o0[j * DH:(j + 1) * DH, :], v[0], pT0[:, j, :, :].rearrange("p b q -> p (b q)"),
                                                start=True, stop=True)
                    done.then_inc(o_psum, 1)
                    for j in range(2):
                        for kb in range(2):
                            done = nc.tensor.matmul(o1[j * DH:(j + 1) * DH, :], v[kb],
                                                    pT1[:, kb, j, :, :].rearrange("p b q -> p (b q)"), start=kb == 0, stop=kb == 1)
                    done.then_inc(o_psum, 1)

                half_chunk(base + 3, 0, [ps[6], ps[7]], between=lambda: (k_transposes(), q_transposes(0)))
                scores(0)
                scores(1)
                half_chunk(base + 4, 1, [ps[6], ps[7]], between=lambda: scores(2))
                scores(3)
                p_transposes(0)
                q_transposes(1)
                for b in range(1, 4):
                    p_transposes(b)
                    scores(b + 3)
                values(0)
                scores(7)
                pe.wait_ge(oT_ready, 1)
                pe.wait_ge(peaks_ready, NB - 1)

                def group_0_parted():
                    p_transposes(4)
                    pe.wait_ge(oT_ready, 2)

                output_slot(base + 5, oT_hi, oT_lo, 0, True, between=group_0_parted)
                p_transposes(5)
                output_slot(base + 6, oT_hi, oT_lo, 2, False, early=lambda: p_transposes(6), between=lambda: p_transposes(7))
                values(1)
                closing(base + 7, oT_hi, oT_lo, 4, ATT_NORM, parted=2)

            def retention():
                base = RET_BASE
                pair = [[ps[0], ps[1]], [ps[2], ps[3]]]

                def rot_transposes(c):
                    pe.wait_ge(rot_ready, 2 * c + 2)
                    if c:
                        pe.wait_ge(rqkT_ready, c)
                    for b in range(4):
                        for t in range(NT):
                            col = (2 * (b % 2) + t) * P
                            done = nc.tensor.transpose(ps[4 + b // 2][:, col:col + P], rot[:, t, b * P:(b + 1) * P], ident[:])
                    done.then_inc(rqkT_psum, 1)

                def ret_scores(h):
                    bank = ps[4 + h]
                    for half in range(2):
                        nc.tensor.matmul(bank[:, 0:256], rqkT[:, 8 + 2 * h + half, 0:P], rqkT[:, 2 * h + half, :],
                                         start=half == 0, stop=half == 1)
                    for half in range(2):
                        done = nc.tensor.matmul(bank[:, 256:384], rqkT[:, 8 + 2 * h + half, P:SEQ],
                                                rqkT[:, 2 * h + half, P:SEQ], start=half == 0, stop=half == 1)
                    done.then_inc(scT_psum, 1)

                def ret_values(h):
                    pe.wait_ge(scT_ready, RH)
                    pe.wait_ge(rv_ready, 2 * h + 2)
                    if h:
                        pe.wait_ge(yn_ready, 2 * h)
                    for bank, c, t, start, stop in ((ps[6], 0, 0, True, True), (ps[7], 1, 0, True, False), (ps[7], 2, 1, False, True)):
                        at = slice(c * P, (c + 1) * P)
                        done = three(bank[:], scT_hi[:, h, at], scT_lo[:, h, at], rv_hi[:, t, :], rv_lo[:, t, :], start, stop)
                    done.then_inc(ry_psum, 1)

                def gated_transposes(h, banks):
                    pe.wait_ge(gated_ready, 2 * h + 2)
                    if h:
                        pe.wait_ge(gT_ready, h)
                    for b in range(4):
                        for t in range(NT):
                            col = (2 * (b % 2) + t) * P
                            done = nc.tensor.transpose(banks[b // 2][:, col:col + P], y_nat[:, t, b * P:(b + 1) * P], ident[:])
                    done.then_inc(gT_psum, 1)

                opening(base, [(BANK, pair[0], [(0, True, False)]), (BANK, pair[0], [(4, False, True)]),
                               (BANK, pair[1], [(0, True, False)])], RET_NORM - 1)
                half_chunk(base + 3, 1, pair[1])
                rot_transposes(0)
                for c in (2, 3):
                    pe.wait_ge(rot_ready, 2 * (c - 2) + 2)
                    half_chunk(base + 2 * c, 0, pair[c % 2])
                    rot_transposes(c - 1)
                    half_chunk(base + 2 * c + 1, 1, pair[c % 2])
                for h in range(RH):
                    if h == 0:
                        pe.wait_ge(rot_ready, 6)
                    else:
                        pe.wait_ge(rv_ready, 2 * h)
                    half_chunk(base + 8 + 4 * h, 0, pair[0])
                    if h == 0:
                        rot_transposes(3)
                    half_chunk(base + 9 + 4 * h, 1, pair[0])
                    if h:
                        gated_transposes(h - 1, [ps[4], ps[5]])
                    if h == 0:
                        pe.wait_ge(rot_ready, 8)
                    else:
                        pe.wait_ge(silu_g_ready, 2 * h)
                    half_chunk(base + 10 + 4 * h, 0, pair[1])
                    if h == 0:
                        pe.wait_ge(rqkT_ready, 4)
                        for head in range(RH):
                            ret_scores(head)
                    else:
                        ret_values(h)
                    half_chunk(base + 11 + 4 * h, 1, pair[1])
                    if h == 0:
                        ret_values(h)
                for d in range(6):
                    pe.wait_ge(gT_ready, RH - 1)
                    pe.wait_ge(yn_ready, 2 * RH)
                    output_slot(base + 24 + d, gT_hi, gT_lo, 2 * d, d == 0)
                    if d == 0:
                        gated_transposes(3, [ps[0], ps[1]])
                pe.wait_ge(gT_ready, RH)
                closing(base + 30, gT_hi, gT_lo, 12, RET_NORM)

            pe.wait_ge(ident_loaded, 16)
            pe.wait_ge(x_loaded[0], 16)
            x_transposes(0, 0, x_nat)
            ffn(0)
            attention()
            ffn(1)
            ffn(2)
            retention()
            ffn(3)

        @block.scalar
        def _(act):
            def split_hi(s, i=0):
                if s >= N_SLOTS:
                    return
                act.wait_ge(raw_loaded[s % RING], 16 * (s // RING + 1) + 16 * i)
                if s >= RING:
                    act.wait_ge(slots_used, used(s - RING) + RING * i)
                at = 0
                if s in HALVED:
                    at = SLOT // 2
                    nc.scalar.activation(w_hi[:, s % RING, 0:at], w_raw[:, s % RING, 0:at], ACT.Copy).then_inc(half_hi, 1)
                nc.scalar.activation(w_hi[:, s % RING, at:], w_raw[:, s % RING, at:], ACT.Copy).then_inc(hi_ready, 1)

            def first_slot_hi(k):
                act.wait_ge(first_raw[k] if k < 3 else raw_loaded[0], 16)
                at = slice(k * BANK, (k + 1) * BANK)
                nc.scalar.activation(w_hi[:, 0, at], w_raw[:, 0, at], ACT.Copy).then_inc(first_hi if k < 3 else hi_ready, 1)

            def first_x_hi(t):
                act.wait_ge(xT_psum, 2 * t + 2)
                pairs = xT_hi[:, :, t * P:(t + 1) * P].rearrange("p (h e k) q -> p h e k q", h=2, e=2)[:, :, 1, :, :]
                nc.scalar.activation(pairs, Y[t][1][:].rearrange("p (h k q) -> p h k q", h=2, k=2), ACT.Copy).then_inc(xT_b_hi, 2)

            def norm_hi(norm, t):
                number = NT * (norm + 1) + t
                act.wait_ge(xT_psum, 2 * number + 2)
                act.wait_ge(xT_b_ready, 2 * number)
                act.wait_ge(cols_loaded, 16)
                for k in (2, 6):
                    for i in range(2):
                        at = ((k - 2) // 2 + i) * P
                        done = nc.scalar.activation(xT_full[:, k + i, :], Y[t][1][:, at:at + P], ACT.Identity,
                                                    bias=cols[:, 1, norm, k + i:k + i + 1], scale=cols[:, 0, norm, k + i:k + i + 1])
                    done.then_inc(xT_b_full, 1)
                    act.wait_ge(xT_b_full, 2 * (NT * norm + t) + k // 4 + 1)
                    nc.scalar.activation(xT_hi[:, k:k + 2, t * P:(t + 1) * P], xT_full[:, k:k + 2, :], ACT.Copy).then_inc(xT_b_hi, 1)

            def ffn(f):
                base = FFN_BASE[f]
                hT_hi, _, silu_gate, _ = ffn_bufs[f]

                def silu(c, i=0):
                    act.wait_ge(slots_used, used(base + 2 * c + 1) + RING * i)
                    if f or c:
                        act.wait_ge(h_ready, 2 * (NCH * f + c) + 4 * i)
                    for t in range(NT):
                        nc.scalar.activation(silu_gate[:, t, :], ps[2 * (c % 2) + t][:, 0:HC], ACT.Silu).then_inc(silu_ready, 1)

                def hidden_hi(c, bank, i=0):
                    act.wait_ge(hT_psum, NCH * f + c + 1 + 2 * i)
                    at = bass.ds(2 * c + 4 * i, 2) if not isinstance(i, int) else slice(2 * c, 2 * c + 2)
                    nc.scalar.activation(hT_hi[:, at, :], bank[:].rearrange("p (b q) -> p b q", b=2), ACT.Copy).then_inc(hT_hi_ready, 1)

                split_hi(base + 3)
                split_hi(base + 4)
                silu(0)
                split_hi(base + 5)
                split_hi(base + 6)
                hidden_hi(0, ps[4])
                with act.Fori(0, 4) as i:
                    for c in (2, 3):
                        silu(c - 1, i)
                        split_hi(base + 2 * c + 3, i)
                        hidden_hi(c - 1, ps[4 + (c - 1) % 2], i)
                        split_hi(base + 2 * c + 4, i)
                silu(NCH - 2)
                split_hi(base + 2 * NCH + 1)
                hidden_hi(NCH - 2, ps[5])
                split_hi(base + 2 * NCH + 2)
                silu(NCH - 1)
                split_hi(base + 2 * NCH + 3)
                hidden_hi(NCH - 1, ps[0])
                for s in range(2 * NCH + 4, FFN_SLOTS + 2):
                    split_hi(base + s)
                ending(FFN_NORM[f])

            def attention_constants():
                act.wait_ge(slots_used, END_SLOT[0])
                act.dma_start(mask[:], mask_in).then_inc(att_consts, 16)
                act.dma_start(bq_col[:], att_cols).then_inc(att_consts, 16)
                act.dma_start(sink[:], sinks).then_inc(att_consts, 16)
                act.dma_start(bv_row[:], att_rows[0:1, D:D + NKV * DH].broadcast_to([P, NKV * DH])).then_inc(att_consts, 16)
                act.dma_start(bo_row[:], att_rows[0:1, 0:D].broadcast_to([P, D])).then_inc(att_consts, 16)

            def retention_constants():
                act.wait_ge(slots_used, END_SLOT[RET_NORM - 1])
                act.dma_start(rope[:], rope_in).then_inc(ret_consts, 16)
                act.dma_start(decay[:], decay_in).then_inc(ret_consts, 16)

            def normalised(norm, t):
                act.wait_ge(shift_ready, NORMED_BY_SCALAR.index((norm, t)) + 1)
                nc.scalar.activation(z[:, t, :], z[:, t, :], ACT.Identity, bias=shift[:, t:t + 1],
                                     scale=rstd[:, t, :]).then_inc(xhat_ready, 2)

            def ending(norm):
                if norm == N_NORMS - 1:
                    return
                if (norm, 0) in NORMED_BY_SCALAR:
                    normalised(norm, 0)
                norm_hi(norm, 0)
                split_hi(END_SLOT[norm] + 2)
                if norm == 0:
                    attention_constants()
                if norm == RET_NORM - 1:
                    retention_constants()
                normalised(norm, 1)
                norm_hi(norm, 1)

            def attention():
                base = ATT_BASE

                def q_copy(n):
                    act.wait_ge(slots_used, used(base + (2, 4)[n]))
                    if n:
                        act.wait_ge(qT_psum, 1)
                    for t in range(NT):
                        done = nc.scalar.activation(q_nat[:, t, :], ps[(2, 6)[n] + t][:], ACT.Copy)
                    done.then_inc(q_nat_ready, 1)

                def exps(b):
                    act.wait_ge(peaks_ready, b + 1)
                    for i, (c, w) in enumerate(((0, 256), (256, 256), (512, P), (640, P))):
                        nc.scalar.activation(probs[:, b % 4, c:c + w], probs[:, b % 4, c:c + w], ACT.Exp, scale=-1.0,
                                             bias=neg_peak[:, b % 4, i:i + 1], accum_out=sums[:, b % 4, i:i + 1])
                    nc.scalar.activation(sink_exp[:, b % 4, :], sink_less[:, b % 4, :], ACT.Exp).then_inc(exps_ready, 1)

                def pT1_copy(b):
                    act.wait_ge(pT_psum, b + 1)
                    if b == 4:
                        act.wait_ge(o_psum, 2)
                    nc.scalar.activation(pT1[:, :, :, b % 4, :].rearrange("p k j q -> p j k q"),
                                         ps[2][:].rearrange("p (j k q) -> p j k q", j=2, k=2), ACT.Copy).then_inc(pT1_ready, 1)

                def o_hi(g):
                    for t in range(NT):
                        act.wait_ge(o_psum, 2 * g + t + 1)
                        nc.scalar.activation(oT_hi[:, 4 * g:4 * g + 4, t * P:(t + 1) * P],
                                             O[g][t][:].rearrange("p (b q) -> p b q", b=4), ACT.Copy).then_inc(oT_hi_ready, 1)

                split_hi(base + 3)
                split_hi(base + 4)
                q_copy(0)
                split_hi(base + 5)
                act.wait_ge(kT_psum, 1)
                act.wait_ge(kz_ready, 1)
                act.wait_ge(att_consts, 16 * 5)
                for g in range(NKV):
                    for j in range(2):
                        rows = slice(j * DH, (j + 1) * DH)
                        done = nc.scalar.activation(kT[rows, g, j, :], ps[0][rows, g * SEQ:(g + 1) * SEQ], ACT.Identity,
                                                    bias=bq_col[rows, NB + g:NB + g + 1])
                done.then_inc(kT_ready, 1)
                split_hi(base + 6)
                exps(0)
                exps(1)
                exps(2)
                q_copy(1)
                pT1_copy(0)
                exps(3)
                pT1_copy(1)
                pT1_copy(2)
                pT1_copy(3)
                exps(4)
                o_hi(0)
                exps(5)
                exps(6)
                pT1_copy(4)
                exps(7)
                pT1_copy(5)
                split_hi(base + 7)
                pT1_copy(6)
                pT1_copy(7)
                split_hi(base + 8)
                split_hi(base + 9)
                o_hi(1)
                split_hi(base + 10)
                ending(ATT_NORM)

            def retention():
                base = RET_BASE

                def rqk_copy(c):
                    act.wait_ge(rqkT_psum, c + 1)
                    for half in range(2):
                        done = nc.scalar.activation(rqkT[:, 4 * c + 2 * half:4 * c + 2 * half + 2, :],
                                                    ps[4 + half][:].rearrange("p (b q) -> p b q", b=2), ACT.Copy)
                    done.then_inc(rqkT_ready, 1)

                def v_copy(h):
                    act.wait_ge(slots_used, used(base + 9 + 4 * h))
                    if h:
                        act.wait_ge(ry_psum, h)
                    for t in range(NT):
                        nc.scalar.activation(rv_hi[:, t, :], ps[t][:], ACT.Copy).then_inc(rv_hi_ready, 1)

                def silu_of_g(h):
                    act.wait_ge(slots_used, used(base + 11 + 4 * h))
                    if h:
                        act.wait_ge(gated_ready, 2 * h)
                    for t in range(NT):
                        nc.scalar.activation(silu_g[:, t, :], ps[2 + t][:], ACT.Silu).then_inc(silu_g_ready, 1)

                def gated_hi(h, banks):
                    act.wait_ge(gT_psum, h + 1)
                    for half in range(2):
                        nc.scalar.activation(gT_hi[:, 4 * h + 2 * half:4 * h + 2 * half + 2, :],
                                             banks[half][:].rearrange("p (b q) -> p b q", b=2), ACT.Copy).then_inc(gT_hi_ready, 1)

                for s in (3, 4, 5, 6):
                    split_hi(base + s)
                rqk_copy(0)
                split_hi(base + 7)
                rqk_copy(1)
                split_hi(base + 8)
                split_hi(base + 9)
                rqk_copy(2)
                split_hi(base + 10)
                split_hi(base + 11)
                rqk_copy(3)
                for h in range(RH):
                    split_hi(base + 12 + 4 * h)
                    v_copy(h)
                    split_hi(base + 13 + 4 * h)
                    if h:
                        gated_hi(h - 1, [ps[4], ps[5]])
                    split_hi(base + 14 + 4 * h)
                    silu_of_g(h)
                    split_hi(base + 15 + 4 * h)
                gated_hi(RH - 1, [ps[0], ps[1]])
                for s in range(28, RET_SLOTS + 2):
                    split_hi(base + s)
                ending(RET_NORM)

            act.dma_start(ident[:], ident_in).then_inc(ident_loaded, 16)
            first_slot_hi(0)
            first_x_hi(0)
            for k in range(1, 4):
                first_slot_hi(k)
            split_hi(1)
            split_hi(2)
            first_x_hi(1)
            ffn(0)
            attention()
            ffn(1)
            ffn(2)
            retention()
            ffn(3)

        @block.vector
        def _(dve):
            def split_lo(s, i=0):
                if s >= N_SLOTS:
                    return
                at = 0
                if s in HALVED:
                    at = SLOT // 2
                    dve.wait_ge(half_hi, HALVED.index(s) + 1)
                    nc.vector.tensor_tensor(w_lo[:, s % RING, 0:at], w_raw[:, s % RING, 0:at], w_hi[:, s % RING, 0:at],
                                            ALU.subtract).then_inc(half_lo, 1)
                dve.wait_ge(hi_ready, s + 1 + RING * i)
                nc.vector.tensor_tensor(w_lo[:, s % RING, at:], w_raw[:, s % RING, at:], w_hi[:, s % RING, at:],
                                        ALU.subtract).then_inc(lo_ready, 1)

            def first_slot_lo(k):
                dve.wait_ge(first_hi if k < 3 else hi_ready, min(k, 2) + 1 if k < 3 else 1)
                at = slice(k * BANK, (k + 1) * BANK)
                nc.vector.tensor_tensor(w_lo[:, 0, at], w_raw[:, 0, at], w_hi[:, 0, at],
                                        ALU.subtract).then_inc(first_lo if k < 3 else lo_ready, 1)

            def both_parts(number, t, k, source):
                at = (slice(None), slice(k, k + 2), slice(t * P, (t + 1) * P))
                nc.vector.tensor_copy(xT_hi[at], source).then_inc(xT_a_hi, 1)
                dve.wait_ge(xT_a_hi, 2 * number + k // 4 + 1)
                nc.vector.tensor_tensor(xT_lo[at], source, xT_hi[at], ALU.subtract).then_inc(xT_a_ready, 1)

            def first_x_a(t, k):
                dve.wait_ge(xT_psum, 2 * t + 1)
                both_parts(t, t, k, Y[t][0][:, k // 2 * P:(k // 2 + 2) * P].rearrange("p (k q) -> p k q", k=2))

            def first_x_b(t, k):
                at = (slice(None), slice(k, k + 2), slice(t * P, (t + 1) * P))
                dve.wait_ge(xT_b_hi, 2 * t + 2)
                nc.vector.tensor_tensor(xT_lo[at], Y[t][1][:, (k // 2 - 1) * P:(k // 2 + 1) * P].rearrange("p (k q) -> p k q", k=2),
                                        xT_hi[at], ALU.subtract).then_inc(xT_b_ready, 1)

            def norm_sum(norm, t, n):
                index = NT * norm + t
                if (t, n) == (1, 1):
                    dve.wait_ge(slots_used, END_SLOT[norm])
                else:
                    dve.wait_ge(y_ready, 3 * norm + 2 * t + n + 1)
                if n == 0 and norm == 0:
                    dve.wait_ge(x_loaded[t], 16)
                elif n == 0:
                    dve.wait_ge(xnat_ready, index - 1)
                if n == 0 and norm == ATT_NORM:
                    dve.wait_ge(res_ready, t + 1)
                half = slice(n * BANK, (n + 1) * BANK)
                nc.vector.scalar_tensor_tensor(z[:, t, half], x_nat[:, t, half], 1.0 if norm == ATT_NORM else ALPHA,
                                               Y[t][n][:], ALU.mult, ALU.add).then_inc(sums_ready, 1)

            def norm_stats(norm, t, n):
                dve.wait_ge(sums_ready, 4 * (NT * norm + t) + 2 * n + 1)
                nc.vector.bn_stats(stats[:, t, n, :], z[:, t, n * BANK:(n + 1) * BANK]).then_inc(sums_ready, 1)

            def norm_moments(norm, t):
                dve.wait_ge(sums_ready, 4 * (NT * norm + t) + 4)
                nc.vector.bn_aggr(moments[:, t, :], stats[:, t, :, :].rearrange("p a b -> p (a b)")).then_inc(stats_ready, 1)

            def norm_apply(norm, t):
                dve.wait_ge(rstd_ready, NT * norm + t + 1)
                for n in range(2):
                    half = slice(n * BANK, (n + 1) * BANK)
                    nc.vector.tensor_scalar(z[:, t, half], z[:, t, half], moments[:, t, 0:1], rstd[:, t, :],
                                            ALU.subtract, ALU.mult).then_inc(xhat_ready, 1)

            def norm_parts(norm, t):
                number = NT * (norm + 1) + t
                dve.wait_ge(xT_psum, 2 * number + 1)
                dve.wait_ge(cols_loaded, 16)
                dve.wait_ge(xT_a_ready, 2 * number)
                for k in (0, 4):
                    for i in (k, k + 1):
                        at = (i - k // 2) * P
                        done = nc.vector.tensor_scalar(xT_full[:, i, :], Y[t][0][:, at:at + P],
                                                       cols[:, 0, norm, i:i + 1], cols[:, 1, norm, i:i + 1], ALU.mult, ALU.add)
                    done.then_inc(xT_a_full, 1)
                    dve.wait_ge(xT_a_full, 2 * (NT * norm + t) + k // 4 + 1)
                    both_parts(number, t, k, xT_full[:, k:k + 2, :])

            def ending(norm):
                if norm == N_NORMS - 1:
                    return
                for n in range(2):
                    norm_sum(norm, 0, n)
                    norm_stats(norm, 0, n)
                norm_moments(norm, 0)
                if norm == ATT_NORM:
                    split_lo(END_SLOT[norm] + 1)
                if (norm, 0) not in NORMED_BY_SCALAR:
                    norm_apply(norm, 0)
                norm_sum(norm, 1, 0)
                norm_parts(norm, 0)
                norm_stats(norm, 1, 0)
                norm_sum(norm, 1, 1)
                norm_stats(norm, 1, 1)
                norm_moments(norm, 1)
                split_lo(END_SLOT[norm] + 2)
                norm_parts(norm, 1)

            def last_norm():
                norm = N_NORMS - 1
                for t in range(NT):
                    for n in range(2):
                        norm_sum(norm, t, n)
                        norm_stats(norm, t, n)
                    norm_moments(norm, t)
                    dve.wait_ge(rows_loaded, 32 * N_NORMS)
                    dve.wait_ge(stats_ready, NT * norm + t + 1)
                    for n in range(2):
                        half = slice(n * BANK, (n + 1) * BANK)
                        nc.vector.scalar_tensor_tensor(z[:, t, half], z[:, t, half], moments[:, t, 0:1], gain_row[:, half],
                                                       ALU.subtract, ALU.mult).then_inc(out_step, 1)
                    dve.wait_ge(rstd_ready, NT * norm + t + 1)
                    for n in range(2):
                        half = slice(n * BANK, (n + 1) * BANK)
                        dve.wait_ge(out_step, 2 * t + n + 1)
                        nc.vector.scalar_tensor_tensor(z[:, t, half], z[:, t, half], rstd[:, t, :], bias_row[:, half],
                                                       ALU.mult, ALU.add).then_inc(out_ready, 1)

            def ffn(f):
                base = FFN_BASE[f]
                hT_hi, hT_lo, silu_gate, h_nat = ffn_bufs[f]

                def gate(c, i=0):
                    if f or c:
                        dve.wait_ge(hT_psum, NCH * f + c + 2 * i)
                    for t in range(NT):
                        dve.wait_ge(silu_ready, 2 * (NCH * f + c) + t + 1 + 4 * i)
                        nc.vector.scalar_tensor_tensor(h_nat[:, t, :], ps[2 * (c % 2) + t][:, HC:2 * HC], 0.5,
                                                       silu_gate[:, t, :], ALU.mult, ALU.mult).then_inc(h_ready, 1)

                def hidden_lo(c, bank, i=0):
                    dve.wait_ge(hT_hi_ready, NCH * f + c + 1 + 2 * i)
                    at = bass.ds(2 * c + 4 * i, 2) if not isinstance(i, int) else slice(2 * c, 2 * c + 2)
                    nc.vector.tensor_tensor(hT_lo[:, at, :], bank[:].rearrange("p (b q) -> p b q", b=2), hT_hi[:, at, :],
                                            ALU.subtract).then_inc(hT_ready, 1)

                split_lo(base + 3)
                split_lo(base + 4)
                gate(0)
                split_lo(base + 5)
                split_lo(base + 6)
                hidden_lo(0, ps[4])
                with dve.Fori(0, 4) as i:
                    for c in (2, 3):
                        gate(c - 1, i)
                        split_lo(base + 2 * c + 3, i)
                        hidden_lo(c - 1, ps[4 + (c - 1) % 2], i)
                        split_lo(base + 2 * c + 4, i)
                gate(NCH - 2)
                split_lo(base + 2 * NCH + 1)
                hidden_lo(NCH - 2, ps[5])
                split_lo(base + 2 * NCH + 2)
                gate(NCH - 1)
                split_lo(base + 2 * NCH + 3)
                hidden_lo(NCH - 1, ps[0])
                for s in range(2 * NCH + 4, FFN_SLOTS + 2):
                    split_lo(base + s)
                ending(FFN_NORM[f])

            def attention():
                base = ATT_BASE
                step = [0]

                def link(instruction):
                    step[0] += 1
                    instruction.then_inc(soft_step, 1)
                    dve.wait_ge(soft_step, step[0])

                def q_scaled(n):
                    dve.wait_ge(qT_psum, n + 1)
                    for b in range(4):
                        done = nc.vector.tensor_scalar(qT[:, 4 * n + b, :], ps[(2, 6)[n] + b // 2][:, (b % 2) * SEQ:(b % 2 + 1) * SEQ],
                                                       bq_col[:, 4 * n + b:4 * n + b + 1], -DH ** -0.5, ALU.add, ALU.mult)
                    done.then_inc(qT_ready, 1)

                def peaks(b):
                    bank1, bank0 = ((ps[4], ps[5]), (ps[0], ps[1]))[b % 2]
                    dve.wait_ge(scores_ready, b + 1)
                    if b >= 4:
                        dve.wait_ge(pT_psum, b - 3)
                    p1 = probs[:, b % 4, 0:512].rearrange("p (j k) -> p j k", j=2)
                    p0 = probs[:, b % 4, 512:768].rearrange("p (j k) -> p j k", j=2)
                    for j in range(2):
                        nc.vector.tensor_tensor_reduce(out=p1[:, j, :], in0=bank1[:, j * 256:(j + 1) * 256], in1=mask[:],
                                                       scale=1.0, scalar=neg_sink[:, b, j:j + 1], op0=ALU.add, op1=ALU.min,
                                                       accum_out=neg_peak[:, b % 4, j:j + 1])
                    for j in range(2):
                        done = nc.vector.tensor_tensor_reduce(out=p0[:, j, :], in0=bank0[:, j * P:(j + 1) * P],
                                                              in1=mask[:, P:2 * P], scale=1.0,
                                                              scalar=neg_sink[:, b, 2 + j:3 + j], op0=ALU.add, op1=ALU.min,
                                                              accum_out=neg_peak[:, b % 4, 2 + j:3 + j])
                    link(done)
                    nc.vector.tensor_tensor(sink_less[:, b % 4, :], neg_peak[:, b % 4, :], neg_sink[:, b, :],
                                            ALU.subtract).then_inc(peaks_ready, 1)

                def totals(b):
                    dve.wait_ge(exps_ready, b + 1)
                    link(nc.vector.tensor_tensor(total[:, b % 4, :], sums[:, b % 4, :], sink_exp[:, b % 4, :], ALU.add))
                    nc.vector.reciprocal(inv[:, b % 4, :], total[:, b % 4, :]).then_inc(inv_ready, 1)

                def pT0_copy(b):
                    dve.wait_ge(pT_psum, b + 1)
                    if b == 4:
                        dve.wait_ge(o_psum, 1)
                    nc.vector.tensor_copy(pT0[:, :, b % 4, :], ps[3][:, 0:256].rearrange("p (j q) -> p j q", j=2)).then_inc(pT0_ready, 1)

                def o_lo(g):
                    for t in range(NT):
                        dve.wait_ge(oT_hi_ready, 2 * g + t + 1)
                        at = (slice(None), slice(4 * g, 4 * g + 4), slice(t * P, (t + 1) * P))
                        nc.vector.tensor_tensor(oT_lo[at], O[g][t][:].rearrange("p (b q) -> p b q", b=4),
                                                oT_hi[at], ALU.subtract).then_inc(oT_ready, 1)

                nc.vector.memset(kT[:], 0.0).then_inc(kz_ready, 1)
                dve.wait_ge(att_consts, 16 * 5)
                link(nc.vector.tensor_scalar(neg_sink[:], sink[:], -1.0, None, ALU.mult))
                split_lo(base + 3)
                dve.wait_ge(slots_used, used(base))
                for t in range(NT):
                    for j in range(2):
                        nc.vector.tensor_copy(k_twice[:, t, :, j, :], ps[t][:, 0:P].rearrange("p (g d) -> p g d", g=NKV))
                    nc.vector.tensor_tensor(v_nat[:, t, :], ps[t][:, P:2 * P], bv_row[:], ALU.add).then_inc(kv_nat, 1)
                split_lo(base + 4)
                q_scaled(0)
                split_lo(base + 5)
                peaks(0)
                peaks(1)
                totals(0)
                peaks(2)
                totals(1)
                peaks(3)
                totals(2)
                pT0_copy(0)
                q_scaled(1)
                totals(3)
                pT0_copy(1)
                pT0_copy(2)
                peaks(4)
                pT0_copy(3)
                peaks(5)
                peaks(6)
                totals(4)
                o_lo(0)
                peaks(7)
                totals(5)
                split_lo(base + 6)
                totals(6)
                pT0_copy(4)
                totals(7)
                pT0_copy(5)
                pT0_copy(6)
                pT0_copy(7)
                split_lo(base + 7)
                split_lo(base + 8)
                o_lo(1)
                split_lo(base + 9)
                ending(ATT_NORM)

            def retention():
                base = RET_BASE
                step = [0]

                def turn(c):
                    dve.wait_ge(slots_used, used(base + 2 * c + 1))
                    if c:
                        dve.wait_ge(rqkT_psum, c)
                    for t in range(NT):
                        halves = ps[2 * (c % 2) + t][:].rearrange("p (h f) -> p h f", f=P)
                        cos, sin = (rope[:, t, j:j + 1, :].broadcast_to([P, 4, P]) for j in range(2))
                        if c or t:
                            dve.wait_ge(rot_ready, 2 * c + t)
                        nc.vector.tensor_tensor(by_cos[:].rearrange("p (h f) -> p h f", f=P), halves, cos, ALU.mult)
                        nc.vector.tensor_tensor(by_sin[:].rearrange("p (h f) -> p h f", f=P), halves, sin,
                                                ALU.mult).then_inc(rot_step, 1)
                        c4, s4, r4 = (a.rearrange("p (h e f) -> p h e f", h=2, e=2) for a in (by_cos[:], by_sin[:], rot[:, t, :]))
                        dve.wait_ge(rot_step, step[0] + 1)
                        nc.vector.tensor_tensor(r4[:, :, 0, :], c4[:, :, 0, :], s4[:, :, 1, :], ALU.subtract).then_inc(rot_step, 1)
                        nc.vector.tensor_tensor(r4[:, :, 1, :], s4[:, :, 0, :], c4[:, :, 1, :], ALU.add).then_inc(rot_ready, 1)
                        step[0] += 2

                def decayed(h):
                    dve.wait_ge(scT_psum, h + 1)
                    nc.vector.tensor_tensor(scT[:, h, :], ps[4 + h][:, 0:384], decay[:, h, :], ALU.mult).then_inc(scT_step, 1)
                    dve.wait_ge(scT_step, 2 * h + 1)
                    nc.vector.tensor_copy(scT_hi[:, h, :], scT[:, h, :]).then_inc(scT_step, 1)
                    dve.wait_ge(scT_step, 2 * h + 2)
                    nc.vector.tensor_tensor(scT_lo[:, h, :], scT[:, h, :], scT_hi[:, h, :], ALU.subtract).then_inc(scT_ready, 1)

                def v_low(h):
                    for t in range(NT):
                        dve.wait_ge(rv_hi_ready, 2 * h + t + 1)
                        nc.vector.tensor_tensor(rv_lo[:, t, :], ps[t][:], rv_hi[:, t, :], ALU.subtract).then_inc(rv_ready, 1)

                def group_stats(h):
                    dve.wait_ge(ry_psum, h + 1)
                    for t in range(NT):
                        nc.vector.bn_stats(gn_stats[:, t, :], ps[6 + t][:]).then_inc(gn_step, 1)
                    for t in range(NT):
                        dve.wait_ge(gn_step, 2 * h + t + 1)
                        nc.vector.bn_aggr(gn_moments[:, t, :], gn_stats[:, t, :]).then_inc(gn_stats_ready, 1)

                def group_norm(h):
                    dve.wait_ge(gn_rstd_ready, 2 * h + 2)
                    if h:
                        dve.wait_ge(gT_psum, h)
                    for t in range(NT):
                        nc.vector.tensor_scalar(y_nat[:, t, :], ps[6 + t][:], gn_moments[:, t, 0:1], gn_rstd[:, t, :],
                                                ALU.subtract, ALU.mult).then_inc(yn_ready, 1)

                def gated(h):
                    for t in range(NT):
                        dve.wait_ge(silu_g_ready, 2 * h + t + 1)
                        dve.wait_ge(yn_ready, 2 * h + t + 1)
                        nc.vector.tensor_tensor(y_nat[:, t, :], y_nat[:, t, :], silu_g[:, t, :], ALU.mult).then_inc(gated_ready, 1)

                def gated_lo(h, banks):
                    for half in range(2):
                        dve.wait_ge(gT_hi_ready, 2 * h + half + 1)
                        at = slice(4 * h + 2 * half, 4 * h + 2 * half + 2)
                        done = nc.vector.tensor_tensor(gT_lo[:, at, :], banks[half][:].rearrange("p (b q) -> p b q", b=2),
                                                       gT_hi[:, at, :], ALU.subtract)
                    done.then_inc(gT_ready, 1)

                split_lo(base + 3)
                split_lo(base + 4)
                dve.wait_ge(ret_consts, 32)
                turn(0)
                split_lo(base + 5)
                turn(1)
                split_lo(base + 6)
                split_lo(base + 7)
                split_lo(base + 8)
                turn(2)
                split_lo(base + 9)
                split_lo(base + 10)
                turn(3)
                split_lo(base + 11)
                for h in range(RH):
                    split_lo(base + 12 + 4 * h)
                    if h == 0:
                        for head in range(RH):
                            decayed(head)
                    v_low(h)
                    split_lo(base + 13 + 4 * h)
                    if h:
                        gated_lo(h - 1, [ps[4], ps[5]])
                    group_stats(h)
                    group_norm(h)
                    split_lo(base + 14 + 4 * h)
                    gated(h)
                    split_lo(base + 15 + 4 * h)
                gated_lo(RH - 1, [ps[0], ps[1]])
                for s in range(28, RET_SLOTS + 2):
                    split_lo(base + s)
                ending(RET_NORM)

            first_slot_lo(0)
            first_x_a(0, 0)
            first_slot_lo(1)
            first_x_b(0, 2)
            first_slot_lo(2)
            first_slot_lo(3)
            first_x_a(0, 4)
            first_x_b(0, 6)
            split_lo(1)
            split_lo(2)
            for k in (0, 4):
                first_x_a(1, k)
                first_x_b(1, k + 2)
            ffn(0)
            attention()
            ffn(1)
            ffn(2)
            retention()
            ffn(3)
            last_norm()

        @block.gpsimd
        def _(pool):
            def rows_for(norm):
                for j, row in enumerate((gain_row, bias_row)):
                    pool.dma_start(row[:], norm_rows[j, norm:norm + 1, :].broadcast_to([P, D])).then_inc(rows_loaded, 16)

            def reciprocal_root(norm, t):
                index = NT * norm + t
                pool.wait_ge(stats_ready, index + 1)
                nc.gpsimd.tensor_tensor(rstd[:, t, :], moments[:, t, 1:2], eps_pow[:, 0:1], ALU.add).then_inc(var_ready, 1)
                pool.wait_ge(var_ready, index + 1)
                nc.gpsimd.tensor_tensor(rstd[:, t, :], rstd[:, t, :], eps_pow[:, 2:3], ALU.pow).then_inc(rstd_ready, 1)

            def low_parts(norm, t):
                number = NT * (norm + 1) + t
                for k in (2, 6):
                    at = (slice(None), slice(k, k + 2), slice(t * P, (t + 1) * P))
                    pool.wait_ge(xT_b_hi, 2 * number + k // 4 + 1)
                    nc.gpsimd.tensor_tensor(xT_lo[at], xT_full[:, k:k + 2, :], xT_hi[at], ALU.subtract).then_inc(xT_b_ready, 1)

            def residual(norm):
                pool.wait_ge(rows_loaded, 32 * (norm + 1))
                for t in range(NT):
                    index = NT * norm + t
                    pool.wait_ge(xhat_ready, 2 * index + 2)
                    nc.gpsimd.tensor_tensor(x_nat[:, t, :], z[:, t, :], gain_row[:], ALU.mult).then_inc(x_scaled, 1)
                    pool.wait_ge(x_scaled, index + 1)
                    nc.gpsimd.tensor_tensor(x_nat[:, t, :], x_nat[:, t, :], bias_row[:], ALU.add).then_inc(xnat_ready, 1)

            def norm_of(norm):
                for t in range(NT):
                    reciprocal_root(norm, t)
                    if (norm, t) in NORMED_BY_SCALAR:
                        pool.wait_ge(rstd_ready, NT * norm + t + 1)
                        nc.gpsimd.tensor_scalar(shift[:, t:t + 1], moments[:, t, 0:1], rstd[:, t, :], -1.0, ALU.mult,
                                                ALU.mult).then_inc(shift_ready, 1)
                    if norm < N_NORMS - 1:
                        low_parts(norm, t)
                if norm < N_NORMS - 1:
                    residual(norm)
                    pool.wait_ge(xnat_ready, NT * (norm + 1))
                    rows_for(norm + 1)

            nc.gpsimd.memset(eps_pow[:, 0:1], LN_EPS)
            nc.gpsimd.memset(eps_pow[:, 1:2], GN_EPS)
            nc.gpsimd.memset(eps_pow[:, 2:3], -0.5).then_inc(eps_ready, 1)
            pool.wait_ge(eps_ready, 1)
            pool.wait_ge(slots_used, 1)
            rows_for(0)
            norm_of(0)
            for b in range(NB):
                pool.wait_ge(inv_ready, b + 1)
                for at, i, w in ((0, 0, 2 * P), (4 * P, 2, P)):
                    p = probs[:, b % 4, at:at + 2 * w].rearrange("p (j k) -> p j k", j=2)
                    done = nc.gpsimd.tensor_tensor(p, p, inv[:, b % 4, i:i + 2, None].broadcast_to([P, 2, w]), ALU.mult)
                done.then_inc(probs_ready, 1)
            pool.wait_ge(att_consts, 16 * 5)
            for t in range(NT):
                pool.wait_ge(xnat_ready, t + 1)
                nc.gpsimd.tensor_scalar(x_nat[:, t, :], x_nat[:, t, :], ALPHA, None, ALU.mult).then_inc(res_scaled, 1)
                pool.wait_ge(res_scaled, t + 1)
                nc.gpsimd.tensor_tensor(x_nat[:, t, :], x_nat[:, t, :], bo_row[:], ALU.add).then_inc(res_ready, 1)
            norm_of(1)
            norm_of(2)
            norm_of(3)
            for h in range(RH):
                for t in range(NT):
                    index = NT * h + t
                    pool.wait_ge(gn_stats_ready, index + 1)
                    nc.gpsimd.tensor_tensor(gn_rstd[:, t, :], gn_moments[:, t, 1:2], eps_pow[:, 1:2], ALU.add).then_inc(gn_var, 1)
                    pool.wait_ge(gn_var, index + 1)
                    nc.gpsimd.tensor_tensor(gn_rstd[:, t, :], gn_rstd[:, t, :], eps_pow[:, 2:3], ALU.pow).then_inc(gn_rstd_ready, 1)
            norm_of(4)
            norm_of(5)


def pack_slots(w, columns):
    import numpy as np
    k = w.shape[0] // P
    blocks = w.reshape(k, P, -1)[:, :, columns]
    per_slot = SLOT // len(columns)
    assert k % per_slot == 0
    return np.transpose(blocks.reshape(k // per_slot, per_slot, P, len(columns)), (0, 2, 1, 3)).reshape(-1, P, SLOT)


def kernel(x, ln_g, ln_b, ffn1_w_gate_up, ffn1_w_down, ffn2_w_gate_up, ffn2_w_down,
           attn_w_qkv, attn_b_qkv, attn_sinks, attn_w_o, attn_b_o, ret_w_qkvg, ret_w_o):
    import numpy as np
    import concourse.bacc as bacc
    from concourse.bass_utils import run_bass_kernel_spmd

    slots = []

    def add_ffn(w_gate_up, w_down):
        for c in range(NCH):
            at = np.arange(c * HC, (c + 1) * HC)
            slots.append(pack_slots(w_gate_up, np.concatenate([at, FFN + at])))
        slots.append(pack_slots(w_down, np.arange(D)))

    add_ffn(ffn1_w_gate_up[0], ffn1_w_down[0])
    slots.append(pack_slots(attn_w_qkv[0], np.arange(D, D + 256)))
    for n in range(2):
        slots.append(pack_slots(attn_w_qkv[0], np.arange(n * BANK, (n + 1) * BANK)))
    slots.append(pack_slots(attn_w_o[0], np.arange(D)))
    add_ffn(ffn2_w_gate_up[0], ffn2_w_down[0])
    add_ffn(ffn1_w_gate_up[1], ffn1_w_down[1])
    order = [0, 1, 2, 3] + [c for h in range(RH) for c in (4 + h, 8 + h)]
    for c in order:
        slots.append(pack_slots(ret_w_qkvg[0], np.arange(c * BANK, (c + 1) * BANK)))
    slots.append(pack_slots(ret_w_o[0], np.arange(D)))
    add_ffn(ffn2_w_gate_up[1], ffn2_w_down[1])
    weights = np.concatenate(slots).reshape(-1, SLOT)
    assert weights.shape[0] == N_SLOTS * P

    norm_rows = np.stack([ln_g.reshape(N_NORMS, D), ln_b.reshape(N_NORMS, D)])
    norm_cols = np.transpose(norm_rows.reshape(2, N_NORMS, KD, P), (3, 0, 1, 2))
    b = attn_b_qkv[0]
    bias_q = b[:D].reshape(NB, P)
    bias_k = b[D:D + NKV * DH].reshape(NKV, 1, DH)
    att_cols = np.concatenate([bias_q, np.repeat(bias_k, 2, axis=1).reshape(NKV, P)]).T
    pairs = attn_sinks[0].reshape(NB, 2)
    sinks = np.broadcast_to(np.concatenate([pairs, pairs], axis=1)[None], (P, NB, 4))
    att_rows = np.concatenate([attn_b_o[0], b[D + NKV * DH:]])[None]

    f = np.float32
    row, col = np.arange(P)[:, None], np.arange(P)[None, :]
    ident = np.eye(P, dtype=f)
    mask = np.concatenate([np.where(col > row, 0.0, 1e30), np.where(col <= row, 0.0, 1e30)], axis=1).astype(f)
    freqs = (f(1.0) / (f(10000.0) ** np.linspace(0.0, 1.0, P, dtype=f))).astype(f)
    angle = (np.arange(SEQ, dtype=f)[:, None] * freqs[None, :]).astype(np.float64)
    rope = np.stack([np.cos(angle), np.sin(angle)], axis=1).astype(f).reshape(NT, P, 2, P).transpose(1, 0, 2, 3)
    gamma = 1.0 - 2.0 ** (-5.0 - np.arange(RH))
    ahead = np.concatenate([col - row, col + P - row, col - row], axis=1)
    decay = np.where(ahead >= 0, gamma[:, None, None] ** np.maximum(ahead, 0), 0.0) * RQ ** -0.5
    decay = decay.transpose(1, 0, 2).astype(f)

    arrays = {"x": x.reshape(SEQ, D), "weights": weights, "norm_rows": norm_rows, "norm_cols": norm_cols,
              "att_cols": att_cols, "sinks": sinks, "att_rows": att_rows, "ident_in": ident, "mask_in": mask,
              "rope_in": rope, "decay_in": decay}
    arrays = {n: np.ascontiguousarray(a) for n, a in arrays.items()}
    nc = bacc.Bacc("TRN2", target_bir_lowering=False, num_devices=1)
    f32 = mybir.dt.float32
    handles = {n: nc.dram_tensor(n, a.shape, f32, kind="ExternalInput").ap() for n, a in arrays.items()}
    out = nc.dram_tensor("out", (SEQ, D), f32, kind="ExternalOutput").ap()
    trunk(nc, out=out, **handles)
    result = run_bass_kernel_spmd(nc, [arrays], core_ids=[0])
    return result.results[0]["out"].reshape(1, SEQ, D)
```
